# Optimizing a Trainium2 kernel written in Bass

```python
import jax, jax.numpy as jnp
from jax import lax
import numpy as np

D_MODEL = 1024
BATCH = 1
SEQ = 256
DEPTH = 2

HEAD_DIM = 64
RWKV_DIM = 3 * D_MODEL // 8
CONV_DIM = D_MODEL // 4
ATTN_DIM = D_MODEL - RWKV_DIM - CONV_DIM
RWKV_HEADS = RWKV_DIM // HEAD_DIM
CONV_GROUPS = CONV_DIM // HEAD_DIM
ATTN_HEADS = ATTN_DIM // HEAD_DIM
DECAY_LORA = 32
ICLR_LORA = 32
VRES_LORA = 16
GATE_LORA = 64
RWKV_IN = 3 * RWKV_DIM + DECAY_LORA + ICLR_LORA + GATE_LORA
CONV_IN = 3 * CONV_DIM
ATTN_IN = 3 * ATTN_DIM
N_IN = RWKV_IN + CONV_IN + ATTN_IN
CONV_WIDTH = 3
DILATED_PATTERNS = ((128, 1), (512, 4), (2048, 16))
ATTN_BLOCK = 128
DIL_SPAN = ATTN_BLOCK * 16
ROPE_THETA = 10000.0
D_FF = 3584
N_EXPERTS = 8
TOP_K = 2
MOE_BLOCK = 128
N_DENSE = (DEPTH + 1) // 2
N_MOE = DEPTH // 2
NORM_EPS = 1e-6
GN_EPS = 64e-5

kernel_name = 'hybrid_rwkv7_shortconv_dilatedattn_moe'

def rms_norm(x, g):
    xf = x.astype(jnp.float32)
    y = xf * lax.rsqrt(jnp.mean(xf * xf, axis=-1, keepdims=True) + NORM_EPS)
    return (y * g.astype(jnp.float32)).astype(x.dtype)

def token_shift(p, mu):
    prev = jnp.pad(p[:, :-1], ((0, 0), (1, 0), (0, 0)))
    return p + (prev - p) * mu

def swiglu(h, wg, wu, wd):
    return (jax.nn.silu(h @ wg) * (h @ wu)) @ wd

def wkv7_scan(r, w, k, v, a, b):
    bsz, _, h, n = r.shape
    xs = tuple(jnp.moveaxis(t, 1, 0) for t in (r, w, k, v, a, b))

    def step(state, inp):
        r_t, w_t, k_t, v_t, a_t, b_t = inp
        sa = jnp.einsum('bhvk,bhk->bhv', state, a_t)
        state = (state * w_t[:, :, None, :] + sa[..., None] * b_t[:, :, None, :]
                 + v_t[..., None] * k_t[:, :, None, :])
        return state, jnp.einsum('bhvk,bhk->bhv', state, r_t)

    state0 = jnp.zeros((bsz, h, n, n), jnp.float32)
    _, ys = lax.scan(step, state0, xs)
    return jnp.moveaxis(ys, 0, 1)

def rwkv7_mix(p, vres, v_first, w0, w2, a0, a2, g2, k_k, k_a, r_k, ln_w, ln_b):
    bsz, seq, _ = p.shape
    p = p.astype(jnp.float32)
    o1, o2, o3 = RWKV_DIM, 2 * RWKV_DIM, 3 * RWKV_DIM
    o4, o5 = o3 + DECAY_LORA, o3 + DECAY_LORA + ICLR_LORA
    r, k, v = p[..., :o1], p[..., o1:o2], p[..., o2:o3]
    wd, ad, gd = p[..., o3:o4], p[..., o4:o5], p[..., o5:]
    log_w = -jax.nn.softplus(-(w0 + jnp.tanh(wd) @ w2)) - 0.5
    decay = jnp.exp(-jnp.exp(log_w))
    a = jax.nn.sigmoid(a0 + ad @ a2)
    g = jax.nn.sigmoid(gd) @ g2
    if vres is None:
        v_first = v
    else:
        pv, v0, v2 = vres
        v = v + (v_first - v) * jax.nn.sigmoid(v0 + pv @ v2)
    heads = lambda t: t.reshape(bsz, seq, RWKV_HEADS, HEAD_DIM)
    kk = heads(k * k_k)
    kk = kk / jnp.maximum(jnp.linalg.norm(kk, axis=-1, keepdims=True), 1e-12)
    k = heads(k * (1.0 + (a - 1.0) * k_a))
    r, v_h, a_h, decay = heads(r), heads(v), heads(a), heads(decay)
    y = wkv7_scan(r, decay, k, v_h, -kk, kk * a_h)
    mean = jnp.mean(y, axis=-1, keepdims=True)
    var = jnp.mean(jnp.square(y - mean), axis=-1, keepdims=True)
    y = ((y - mean) * lax.rsqrt(var + GN_EPS)).reshape(bsz, seq, RWKV_DIM) * ln_w + ln_b
    bonus = jnp.sum(r * k * r_k, axis=-1, keepdims=True) * v_h
    out = (y + bonus.reshape(bsz, seq, RWKV_DIM)) * g
    return out, v_first

def short_conv_mix(p, conv_w, out_gain):
    bsz, seq, _ = p.shape
    b_gate, c_gate, xc = p[..., :CONV_DIM], p[..., CONV_DIM:2 * CONV_DIM], p[..., 2 * CONV_DIM:]
    u = c_gate * xc
    filt = conv_w.astype(u.dtype)[:, None, :]
    y = lax.conv_general_dilated(u, filt, window_strides=(1,), padding=[(CONV_WIDTH - 1, 0)],
                                 dimension_numbers=('NWC', 'WIO', 'NWC'),
                                 feature_group_count=CONV_DIM)
    y = (b_gate * y).reshape(bsz, seq, CONV_GROUPS, HEAD_DIM)
    return rms_norm(y, out_gain).reshape(bsz, seq, CONV_DIM)

def rope(x):
    seq, dim = x.shape[1], x.shape[-1]
    half = dim // 2
    inv_freq = ROPE_THETA ** (-jnp.arange(half, dtype=jnp.float32) * 2.0 / dim)
    ang = jnp.arange(seq, dtype=jnp.float32)[:, None] * inv_freq[None, :]
    cos = jnp.cos(ang)[None, :, None, :]
    sin = jnp.sin(ang)[None, :, None, :]
    xf = x.astype(jnp.float32)
    x1, x2 = xf[..., :half], xf[..., half:]
    return jnp.concatenate([x1 * cos - x2 * sin, x2 * cos + x1 * sin], axis=-1).astype(x.dtype)

def to_dilated(x, dil):
    bsz, sp, h, d = x.shape
    return x.reshape(bsz, sp // dil, dil, h, d).transpose(0, 2, 3, 1, 4).reshape(bsz * dil, h, sp // dil, d)

def from_dilated(y, dil, bsz):
    _, h, l, d = y.shape
    return y.reshape(bsz, dil, h, l, d).transpose(0, 3, 1, 2, 4).reshape(bsz, l * dil, h, d)

def banded_attention(q, k, v, n_back):
    n, h, l, d = q.shape
    nb, blk = l // ATTN_BLOCK, ATTN_BLOCK
    f32 = jnp.float32
    to_blocks = lambda t: t.astype(f32).reshape(n, h, nb, blk, d)
    qb, kb, vb = to_blocks(q), to_blocks(k), to_blocks(v)
    prev = lambda t: jnp.pad(t[:, :, :-1], ((0, 0), (0, 0), (1, 0), (0, 0), (0, 0)))
    kw = jnp.concatenate([prev(kb), kb], axis=3)
    vw = jnp.concatenate([prev(vb), vb], axis=3)
    s = jnp.einsum('nhbqd,nhbkd->nhbqk', qb, kw) * (d ** -0.5)
    qi = jnp.arange(blk)[:, None]
    kj = jnp.arange(2 * blk)[None, :]
    dist = qi + blk - kj
    band = (dist >= 0) & (dist <= n_back)
    has_prev = (jnp.arange(nb)[:, None, None] > 0) | (kj >= blk)[None]
    mask = band[None] & has_prev
    s = jnp.where(mask, s, -jnp.inf)
    m = jnp.max(s, axis=-1, keepdims=True)
    pexp = jnp.exp(s - m)
    den = jnp.sum(pexp, axis=-1, keepdims=True)
    o = jnp.einsum('nhbqk,nhbkd->nhbqd', pexp, vw) / den
    lse = (m + jnp.log(den))[..., 0]
    return o.reshape(n, h, l, d), lse.reshape(n, h, l)

def dilated_attention_mix(p, q_gain, k_gain, out_gain):
    bsz, seq, _ = p.shape
    part = lambda i: p[..., i * ATTN_DIM:(i + 1) * ATTN_DIM].reshape(bsz, seq, ATTN_HEADS, HEAD_DIM)
    q = rope(rms_norm(part(0), q_gain))
    k = rope(rms_norm(part(1), k_gain))
    v = part(2)
    s_pad = -(-seq // DIL_SPAN) * DIL_SPAN
    padw = ((0, 0), (0, s_pad - seq), (0, 0), (0, 0))
    q, k, v = jnp.pad(q, padw), jnp.pad(k, padw), jnp.pad(v, padw)
    outs, lses = [], []
    for window, dil in DILATED_PATTERNS:
        o, lse = banded_attention(to_dilated(q, dil), to_dilated(k, dil), to_dilated(v, dil), window // dil)
        outs.append(from_dilated(o, dil, bsz)[:, :seq])
        lses.append(from_dilated(lse[..., None], dil, bsz)[:, :seq, :, 0])
    wts = jax.nn.softmax(jnp.stack(lses), axis=0)
    o = jnp.einsum('pbsh,pbshd->bshd', wts, jnp.stack(outs))
    o = rms_norm(o.astype(p.dtype), out_gain)
    return o.reshape(bsz, seq, ATTN_DIM)

def moe_swiglu(h, router, wg, wu, wd):
    bsz, seq, d = h.shape
    t = bsz * seq
    xt = h.reshape(t, d)
    logits = (xt @ router).astype(jnp.float32)
    topv, topi = lax.top_k(logits, TOP_K)
    gates = jax.nn.softmax(topv, axis=-1)
    flat_e = topi.reshape(-1)
    flat_tok = jnp.repeat(jnp.arange(t, dtype=jnp.int32), TOP_K)
    flat_g = gates.reshape(-1)
    order = jnp.argsort(flat_e)
    se = flat_e[order]
    counts = jnp.bincount(flat_e, length=N_EXPERTS)
    padded = (counts + MOE_BLOCK - 1) // MOE_BLOCK * MOE_BLOCK
    start = jnp.cumsum(counts) - counts
    ends_p = jnp.cumsum(padded)
    pstart = ends_p - padded
    dest = pstart[se] + (jnp.arange(t * TOP_K) - start[se])
    n_rows = t * TOP_K + N_EXPERTS * MOE_BLOCK
    row_tok = jnp.full((n_rows,), t, jnp.int32).at[dest].set(flat_tok[order])
    row_gate = jnp.zeros((n_rows,), jnp.float32).at[dest].set(flat_g[order])
    n_blocks = n_rows // MOE_BLOCK
    block_expert = jnp.minimum(
        jnp.searchsorted(ends_p, jnp.arange(n_blocks) * MOE_BLOCK, side='right'), N_EXPERTS - 1)
    xpad = jnp.concatenate([xt, jnp.zeros((1, d), xt.dtype)], axis=0)
    xb = xpad[row_tok].reshape(n_blocks, MOE_BLOCK, d)

    def expert_block(args):
        xblk, e = args
        return swiglu(xblk, wg[e], wu[e], wd[e])

    yb = lax.map(expert_block, (xb, block_expert))
    y = (yb.reshape(n_rows, d) * row_gate[:, None]).astype(h.dtype)
    out = jnp.zeros((t + 1, d), h.dtype).at[row_tok].add(y)[:t]
    return out.reshape(bsz, seq, d)

def setup_inputs(seed: int = 0) -> dict:
    key = jax.random.key(seed)
    ks = jax.random.split(key, 32)
    f32 = jnp.float32
    L = DEPTH
    nrm = lambda i, shape, scale: scale * jax.random.normal(ks[i], shape, f32)
    gain = lambda i, shape: 1.0 + nrm(i, shape, 0.02)
    unif = lambda i, shape, lo, hi: jax.random.uniform(ks[i], shape, f32, lo, hi)
    return {
        'x': nrm(0, (BATCH, SEQ, D_MODEL), 1.0),
        'mix_norm': gain(1, (L, D_MODEL)),
        'w_in': nrm(2, (L, D_MODEL, N_IN), D_MODEL ** -0.5),
        'tshift_mu': unif(3, (L, RWKV_IN), 0.0, 1.0),
        'vres_w_in': nrm(4, (L - 1, D_MODEL, VRES_LORA), D_MODEL ** -0.5),
        'vres_mu': unif(5, (L - 1, VRES_LORA), 0.0, 1.0),
        'vres_v0': 1.0 + nrm(6, (L - 1, RWKV_DIM), 0.3),
        'vres_v2': nrm(7, (L - 1, VRES_LORA, RWKV_DIM), VRES_LORA ** -0.5),
        'decay_w0': unif(8, (L, RWKV_DIM), -5.0, -0.5),
        'decay_w2': nrm(9, (L, DECAY_LORA, RWKV_DIM), 0.5 * DECAY_LORA ** -0.5),
        'iclr_a0': nrm(10, (L, RWKV_DIM), 0.5),
        'iclr_a2': nrm(11, (L, ICLR_LORA, RWKV_DIM), 0.5 * ICLR_LORA ** -0.5),
        'gate_g2': nrm(12, (L, GATE_LORA, RWKV_DIM), GATE_LORA ** -0.5),
        'k_k': 0.85 + nrm(13, (L, RWKV_DIM), 0.1),
        'k_a': 1.0 + nrm(14, (L, RWKV_DIM), 0.1),
        'r_k': nrm(15, (L, RWKV_HEADS, HEAD_DIM), 0.1),
        'ln_x_w': gain(16, (L, RWKV_DIM)),
        'ln_x_b': nrm(17, (L, RWKV_DIM), 0.02),
        'conv_w': nrm(18, (L, CONV_WIDTH, CONV_DIM), CONV_WIDTH ** -0.5),
        'conv_out_norm': gain(19, (L, CONV_GROUPS, HEAD_DIM)),
        'q_norm': gain(20, (L, HEAD_DIM)),
        'k_norm': gain(21, (L, HEAD_DIM)),
        'attn_out_norm': gain(22, (L, ATTN_HEADS, HEAD_DIM)),
        'w_o': nrm(23, (L, D_MODEL, D_MODEL), D_MODEL ** -0.5),
        'ffn_norm': gain(24, (L, D_MODEL)),
        'dense_wg': nrm(25, (N_DENSE, D_MODEL, D_FF), D_MODEL ** -0.5),
        'dense_wu': nrm(26, (N_DENSE, D_MODEL, D_FF), D_MODEL ** -0.5),
        'dense_wd': nrm(27, (N_DENSE, D_FF, D_MODEL), D_FF ** -0.5),
        'router': nrm(28, (N_MOE, D_MODEL, N_EXPERTS), D_MODEL ** -0.5),
        'moe_wg': nrm(29, (N_MOE, N_EXPERTS, D_MODEL, D_FF), D_MODEL ** -0.5),
        'moe_wu': nrm(30, (N_MOE, N_EXPERTS, D_MODEL, D_FF), D_MODEL ** -0.5),
        'moe_wd': nrm(31, (N_MOE, N_EXPERTS, D_FF, D_MODEL), D_FF ** -0.5),
    }

def reference(x, mix_norm, w_in, tshift_mu, vres_w_in, vres_mu, vres_v0, vres_v2,
              decay_w0, decay_w2, iclr_a0, iclr_a2, gate_g2, k_k, k_a, r_k, ln_x_w, ln_x_b,
              conv_w, conv_out_norm, q_norm, k_norm, attn_out_norm, w_o, ffn_norm,
              dense_wg, dense_wu, dense_wd, router, moe_wg, moe_wu, moe_wd):
    v_first = None
    for l in range(DEPTH):
        h = rms_norm(x, mix_norm[l])
        if l == 0:
            w_comb = w_in[l]
        else:
            w_comb = jnp.concatenate([w_in[l], vres_w_in[l - 1]], axis=1)
        p = h @ w_comb
        p_rwkv = token_shift(p[..., :RWKV_IN], tshift_mu[l])
        p_conv = p[..., RWKV_IN:RWKV_IN + CONV_IN]
        p_attn = p[..., RWKV_IN + CONV_IN:N_IN]
        if l == 0:
            vres = None
        else:
            vres = (token_shift(p[..., N_IN:], vres_mu[l - 1]), vres_v0[l - 1], vres_v2[l - 1])
        y_rwkv, v_first = rwkv7_mix(p_rwkv, vres, v_first, decay_w0[l], decay_w2[l], iclr_a0[l],
                                    iclr_a2[l], gate_g2[l], k_k[l], k_a[l], r_k[l],
                                    ln_x_w[l], ln_x_b[l])
        y_conv = short_conv_mix(p_conv, conv_w[l], conv_out_norm[l])
        y_attn = dilated_attention_mix(p_attn, q_norm[l], k_norm[l], attn_out_norm[l])
        y = jnp.concatenate([y_rwkv.astype(x.dtype), y_conv, y_attn], axis=-1)
        x = x + y @ w_o[l]
        h = rms_norm(x, ffn_norm[l])
        if l % 2 == 0:
            i = l // 2
            x = x + swiglu(h, dense_wg[i], dense_wu[i], dense_wd[i])
        else:
            i = l // 2
            x = x + moe_swiglu(h, router[i], moe_wg[i], moe_wu[i], moe_wd[i])
    return x


_drawn_inputs = setup_inputs


def setup_inputs(seed=0):
    import zlib

    import numpy as np

    out = dict(_drawn_inputs(seed))
    spreads = {}
    factors = {'ln_x_w': 3.61,
     'ln_x_b': 4.571,
     'conv_out_norm': 3.255,
     'q_norm': 3.458,
     'k_norm': 3.63,
     'attn_out_norm': 3.399,
     'ffn_norm': 3.099}
    for name, (base, spread) in spreads.items():
        noise = np.random.default_rng([zlib.crc32(name.encode()), seed]).standard_normal(out[name].shape)
        drawn = base * np.exp(spread * noise) if base else spread * noise
        out[name] = __import__('jax').numpy.asarray(drawn.astype(out[name].dtype))
    for name, factor in factors.items():
        out[name] = (out[name] * factor).astype(out[name].dtype)
    return out
```

```python
from contextlib import ExitStack

import numpy as np

import concourse.bass as bass
from concourse import mybir

F32 = mybir.dt.float32
F32R = mybir.dt.float32r
I32 = mybir.dt.int32
U8 = mybir.dt.uint8
ALU = mybir.AluOpType
ACT = mybir.ActivationFunctionType
AX = mybir.AxisListType

P = 128
D = 1024
T = 256
L = 2
KT = D // P
RW = 384
NRT = RW // P
HEADS = 6
HD = 64
N_IN = 3200
F = 3584
NE = 8
C = 64
NC = T // C
CW = 512
NJ = F // CW
HALF = KT * CW // 2
SLOTS = 7
FIRST_OVER = 4
PIECE = HALF // 2
PIECES = 4
NORM_EPS = 1e-6
GN_EPS = 64e-5
DECAY = float(np.exp(-0.5))
SEL_ROWS = 12

CONST_COLS = {}
_at = 0
for _name, _n in (("ident", P), ("ones", P), ("pair", P), ("rot", P), ("cos", T), ("sin", T), ("strict", P),
                  ("incl", P), ("bias", 3 * P), ("iota", P), ("tri", P), ("selin", 6 * SEL_ROWS), ("selout", 6 * P)):
    CONST_COLS[_name] = (_at, _n)
    _at += _n
N_CONST = _at

PARAM_COLS = {}
_at = 0
for _name, _n in (("mix_norm", 8), ("mu", 10), ("w0", 3), ("a0", 3), ("k_k", 3), ("k_a", 3), ("r_k", 3), ("ln_w", 3),
                  ("ln_b", 3), ("conv_w", 6), ("conv_g", 2), ("q_g", 1), ("k_g", 1), ("out_g", 3), ("ffn_norm", 8),
                  ("vres_mu", 1), ("vres_v0", 3)):
    PARAM_COLS[_name] = (_at, _n)
    _at += _n
N_PARAM = _at


def constant_tables():
    c = np.zeros((P, N_CONST), np.float32)

    def put(name, a):
        at, n = CONST_COLS[name]
        c[:a.shape[0], at:at + n] = a

    i = np.arange(P)
    put("ident", np.eye(P))
    put("ones", np.ones((P, P)))
    put("pair", i[:, None] // HD == i[None, :] // HD)
    rot = np.zeros((P, P))
    for m in range(P):
        if m % HD < HD // 2:
            rot[m + HD // 2, m] = -1.0
        else:
            rot[m - HD // 2, m] = 1.0
    put("rot", rot)
    inv_freq = np.float32(10000.0) ** (-np.arange(HD // 2, dtype=np.float32) * np.float32(2.0) / np.float32(HD))
    ang = np.arange(T, dtype=np.float32)[None, :] * inv_freq.astype(np.float32)[i % (HD // 2)][:, None]
    put("cos", np.cos(ang))
    put("sin", np.sin(ang))
    same = i[:, None] // C == i[None, :] // C
    put("strict", same & (i[:, None] < i[None, :]))
    put("incl", same & (i[:, None] <= i[None, :]))
    q, k = np.arange(T)[:, None], np.arange(T)[None, :]
    seen = np.zeros((T, T))
    for window, dil in ((128, 1), (512, 4), (2048, 16)):
        seen += (q >= k) & (q - k <= window) & ((q - k) % dil == 0)
    bias = np.where(seen > 0, np.log(np.maximum(seen, 1)), -1e30)
    put("bias", np.concatenate([bias[:P, :P], bias[P:, :]], axis=1))
    put("iota", np.tile(i, (P, 1)))
    put("tri", i[:, None] < i[None, :])
    selin = np.zeros((P, 6, SEL_ROWS))
    selout = np.zeros((SEL_ROWS, 6, P))
    for t in range(6):
        for m in range(P):
            selin[m, t, 2 * t + m // HD] = 1.0
            selout[2 * t + m // HD, t, m] = 1.0
    put("selin", selin.reshape(P, -1))
    put("selout", selout.reshape(SEL_ROWS, -1))
    masks = np.zeros((P, 2, 6, P), np.float32)
    for lev in range(6):
        b = 1 << lev
        m = (i[:, None] // (2 * b) == i[None, :] // (2 * b)) & (i[:, None] // b % 2 == 1) & (i[None, :] // b % 2 == 0)
        masks[:, 0, lev] = m
        masks[:, 1, lev] = m.T
    return c, masks.reshape(P, -1)


def decoder_trunk(nc, x, consts, masks, params, lora, vres_v2, w_in, vres_w, w_o, dense_wg, dense_wu, dense_wd,
                  router, moe_wg, moe_wu, moe_wd, out):
    with ExitStack() as ctx:
        def sem(name):
            return ctx.enter_context(nc.semaphore(name))

        ring = ctx.enter_context(nc.sbuf_tensor("ring", [P, SLOTS, HALF], F32))
        ARENA = 26100
        arena = ctx.enter_context(nc.sbuf_tensor("arena", [P, ARENA], F32))
        mask8 = ctx.enter_context(nc.sbuf_tensor("mask8", [P, 12 * P], U8))
        flag = ctx.enter_context(nc.sbuf_tensor("flag", [P, 1], I32))
        w_hi = ctx.enter_context(nc.sbuf_tensor("w_hi", [P, PIECES, PIECE], F32R))
        w_lo = ctx.enter_context(nc.sbuf_tensor("w_lo", [P, PIECES, PIECE], F32R))
        xg_hi = ctx.enter_context(nc.sbuf_tensor("xg_hi", [P, KT * P], F32R))
        xg_lo = ctx.enter_context(nc.sbuf_tensor("xg_lo", [P, KT * P], F32R))
        at_hi = ctx.enter_context(nc.sbuf_tensor("at_hi", [P, 2, CW], F32R))
        at_lo = ctx.enter_context(nc.sbuf_tensor("at_lo", [P, 2, CW], F32R))
        bank = [ctx.enter_context(nc.psum_tensor(f"bank{b}", [P, 512], F32)) for b in range(8)]

        class Region:

            def __init__(self, ap, size):
                self.ap, self.size, self.at = ap, size, 0

            def take(self, n):
                a = self.at
                self.at += n
                assert self.at <= self.size, (self.at, self.size)
                return self.ap[:, a:a + n]

        keep = Region(arena[:, :], ARENA)
        cst = keep.take(N_CONST)
        prm = keep.take(L * N_PARAM)
        lora_w = keep.take(L * RW).rearrange("p (l n) -> p l n", l=L)
        v2w = keep.take(RW)
        vres_wt = keep.take(KT * 16).rearrange("p (k n) -> p k n", k=KT)
        router_w = keep.take(KT * NE).rearrange("p (k n) -> p k n", k=KT)
        xT = keep.take(KT * T).rearrange("p (k t) -> p k t", k=KT)
        hT = keep.take(KT * T).rearrange("p (k t) -> p k t", k=KT)
        rn = keep.take(T)
        small = keep.take(320)
        top_gap = small[:, 160:162]
        phase = keep.at

        pT = keep.take(22 * T).rearrange("p (k t) -> p k t", k=22)
        v_att = keep.take(2 * RW).rearrange("p (b n) -> p b n", b=2)
        v_first = keep.take(NRT * T).rearrange("p (i t) -> p i t", i=NRT)
        w65 = keep.take(NRT * NC * (C + 1)).rearrange("p (i c t) -> p i c t", i=NRT, c=NC)
        gram = [keep.take(HEADS * P).rearrange("p (h t) -> p h t", h=HEADS) for _ in range(4)]
        inv_w, a_gate, tmp1, tmp2 = [g.rearrange("p h t -> p (h t)").rearrange("p (i t) -> p i t", i=NRT)
                                     for g in gram]
        g_gate = keep.take(NRT * T).rearrange("p (i t) -> p i t", i=NRT)
        bonus = keep.take(NRT * T).rearrange("p (i t) -> p i t", i=NRT)
        tok_all = keep.take(4 * RW)
        tok = [tok_all[:, n * RW:(n + 1) * RW] for n in range(4)]
        lora_in = keep.take(T)
        pv = keep.take(T)
        state = arena[:, keep.at - 2 * T:keep.at - 2 * T + RW].rearrange("p (i v) -> p i v", i=NRT)
        head_rn = keep.take(T)
        sq_qk = keep.take(6 * T).rearrange("p (k t) -> p k t", k=6)
        o_tok = sq_qk.rearrange("p k t -> p (k t)")[:, 0:2 * RW].rearrange("p (b h d) -> p b h d", b=2, h=HEADS)
        o_sq = sq_qk.rearrange("p k t -> p (k t)")[:, 2 * RW:4 * RW].rearrange("p (b h d) -> p b h d", b=2, h=HEADS)
        probs = [keep.take(3 * P) for _ in range(2)]
        assert keep.at <= ARENA
        kk = tok_all[:, 0:2 * RW].rearrange("p (i t) -> p i t", i=NRT)
        sig_w = tok_all[:, 2 * RW:4 * RW].rearrange("p (i t) -> p i t", i=NRT)
        aT = hT[:, 0:3, :]
        bT = hT[:, 3:6, :]

        over = Region(ring[:, FIRST_OVER:SLOTS, :].rearrange("p s n -> p (s n)"), (SLOTS - FIRST_OVER) * HALF)
        inv = over.take(HEADS * P).rearrange("p (h t) -> p h t", h=HEADS)
        invT = over.take(HEADS * P).rearrange("p (h t) -> p h t", h=HEADS)
        lt = over.take(HEADS * P).rearrange("p (h t) -> p h t", h=HEADS)
        lv = over.take(RW)
        p1 = over.take(RW)
        u_tok = over.take(RW)
        y_cross = over.take(RW)
        y_tok = over.take(RW)
        state_tmp = over.take(RW).rearrange("p (i v) -> p i v", i=NRT)
        end_w = over.take(RW).rearrange("p (i v) -> p i v", i=NRT)
        ta_t = over.take(RW).rearrange("p (i t) -> p i t", i=NRT)
        probs_t = over.take(3 * P)
        conv_tmp = over.take(T)
        moe = Region(arena[:, phase:ARENA], ARENA - phase)
        x_tok = moe.take(2 * D).rearrange("p (b d) -> p b d", b=2)
        h_tok = moe.take(2 * D).rearrange("p (b d) -> p b d", b=2)
        onehot = moe.take(2 * NE * P).rearrange("p (b e s) -> p b e s", b=2, e=NE)
        gated = moe.take(2 * NE * P).rearrange("p (b e s) -> p b e s", b=2, e=NE)
        combine = moe.take(NE * T).rearrange("p (e t) -> p e t", e=NE)
        combine_e = moe.take(T)
        act_b = [moe.take(CW) for _ in range(2)]
        sil_b = [moe.take(CW) for _ in range(2)]
        dense = Region(arena[:, phase:ARENA], ARENA - phase)
        dense_act = [dense.take(T) for _ in range(8)]
        dense_sil = [dense.take(T) for _ in range(2)]
        mask_in = h_tok.rearrange("p b d -> p (b d)")[:, 0:12 * P]
        gated_all = gated.rearrange("p b e s -> p (b e s)")
        yg = gated_all[:, D:2 * D]

        def const(name, rows=P):
            at, n = CONST_COLS[name]
            return cst[0:rows, at:at + n]

        def param(l, name, i=0):
            at = l * N_PARAM + PARAM_COLS[name][0] + i
            return prm[:, at:at + 1]

        def spread(ap, n):
            return ap.rearrange("p (a m) -> p a m", a=1).to_broadcast([ap.shape[0], n, ap.shape[1]])

        def stretch(ap, n):
            return ap.rearrange("p (m a) -> p m a", a=1).to_broadcast([ap.shape[0], ap.shape[1], n])

        def lane(h):
            return h % 2 * 3 + h // 2

        ident = const("ident")
        ones = const("ones")
        selin = const("selin").rearrange("p (t m) -> p t m", t=6)
        selout = const("selout", SEL_ROWS).rearrange("p (t m) -> p t m", t=6)
        lmask = mask8[:, :].rearrange("p (a l m) -> p a l m", a=2, l=6)

        inputs_in = sem("inputs_in")
        ring_in = [sem(f"ring_in{s}") for s in range(SLOTS)]
        hi_ready = sem("hi_ready")
        lo_ready = sem("lo_ready")
        pc_free = sem("pc_free")
        x_turned = sem("x_turned")
        x_kept = sem("x_kept")
        sq_ready = sem("sq_ready")
        ss_ready = sem("ss_ready")
        ms_ready = sem("ms_ready")
        rn_ready = sem("rn_ready")
        h_ready = sem("h_ready")
        unit_done = sem("unit_done")
        unit_kept = sem("unit_kept")
        lora_ready = sem("lora_ready")
        vres_shifted = sem("vres_shifted")
        lora_act = sem("lora_act")
        lora_done = sem("lora_done")
        lora_kept = sem("lora_kept")
        cs_ready = sem("cs_ready")
        w_ready = sem("w_ready")
        hs_sq = sem("hs_sq")
        hs_sum = sem("hs_sum")
        hs_rec = sem("hs_rec")
        hs_root = sem("hs_root")
        hs_bc = sem("hs_bc")
        hs_used = sem("hs_used")
        qk_sq = sem("qk_sq")
        bonus_in = sem("bonus_in")
        bonus_sum = sem("bonus_sum")
        bonus_ready = sem("bonus_ready")
        rw_ready = sem("rw_ready")
        rot_done = sem("rot_done")
        rope_ready = sem("rope_ready")
        state_zero = sem("state_zero")
        inv_init = sem("inv_init")
        tok_done = sem("tok_done")
        tok_kept_a = sem("tok_kept_a")
        tok_kept_d = sem("tok_kept_d")
        gram_done = sem("gram_done")
        gram_kept = sem("gram_kept")
        lv_done = sem("lv_done")
        lv_kept = sem("lv_kept")
        lt_done = sem("lt_done")
        lt_kept = sem("lt_kept")
        tlt_done = sem("tlt_done")
        inv_ready = sem("inv_ready")
        p1_done = sem("p1_done")
        p1_kept = sem("p1_kept")
        ta_kept = sem("ta_kept")
        u_done = sem("u_done")
        u_ready = sem("u_ready")
        yc_done = sem("yc_done")
        yc_kept = sem("yc_kept")
        st_done = sem("st_done")
        st_ready = sem("st_ready")
        y_done = sem("y_done")
        gn_rec = sem("gn_rec")
        gn_root = sem("gn_root")
        yn_ready = sem("yn_ready")
        yt_done = sem("yt_done")
        y_out = sem("y_out")
        sc_done = sem("sc_done")
        sc_read = sem("sc_read")
        mx_ready = sem("mx_ready")
        ex_done = sem("ex_done")
        tp_done = sem("tp_done")
        tp_kept = sem("tp_kept")
        pv_done = sem("pv_done")
        o_ready = sem("o_ready")
        on_rec = sem("on_rec")
        on_root = sem("on_root")
        on_ready = sem("on_ready")
        ot_done = sem("ot_done")
        att_out = sem("att_out")
        wo_done = sem("wo_done")
        wo_added = sem("wo_added")
        dg_done = sem("dg_done")
        ds_done = sem("ds_done")
        da_ready = sem("da_ready")
        dd_done = sem("dd_done")
        x_ffn = sem("x_ffn")
        logit_done = sem("logit_done")
        pe_turned = sem("pe_turned")
        act_turned = sem("act_turned")
        route_sel = sem("route_sel")
        rank_done = sem("rank_done")
        route_act = sem("route_act")
        route_exp = sem("route_exp")
        flag_ready = sem("flag_ready")
        oh_ready = sem("oh_ready")
        cb_done = sem("cb_done")
        cb_kept = sem("cb_kept")
        ga_done = sem("ga_done")
        ga_kept = sem("ga_kept")
        ga_low = sem("ga_low")
        gt_done = sem("gt_done")
        up_done = sem("up_done")
        sl_done = sem("sl_done")
        ac_ready = sem("ac_ready")
        at_done = sem("at_done")
        at_kept = sem("at_kept")
        at_low = sem("at_low")
        dn_done = sem("dn_done")
        yg_kept = sem("yg_kept")
        cbe_ready = sem("cbe_ready")
        sct_done = sem("sct_done")
        sct_added = sem("sct_added")
        moe_done = sem("moe_done")
        out_done = sem("out_done")
        dve_step = sem("dve_step")
        act_step = sem("act_step")
        pool_step = sem("pool_step")

        CHUNKS = (4, 5, 6, 2, 0, 1, 3)
        N_UNITS = (26, 27)
        UNIT0 = (0, 26)
        LORAS = (3, 4)
        LORA0 = (0, 3)

        def units(l):
            got = []
            for place, ch in enumerate(CHUNKS):
                mine = [("cm", n) for n in range(4 * ch, 4 * ch + 4) if n < 22]
                if ch == 5:
                    mine += [("va", 0), ("va", 1)]
                if ch == 6:
                    mine = [("vb", 0), ("vb", 1)] + ([("vres", 0)] if l else [])
                got += [(place, *m, i == 0, i == len(mine) - 1) for i, m in enumerate(mine)]
            return got

        def kept(l, kind, n):
            return UNIT0[l] + [u[1:3] for u in units(l)].index((kind, n)) + 1

        ORDER = [("g", 0), ("u", 0)]
        for _j in range(1, NJ):
            ORDER += [("g", _j), ("u", _j), ("d", _j - 1)]
        ORDER += [("d", NJ - 1)]

        stream = []
        for l in range(L):
            us = units(l)
            for place, ch in enumerate(CHUNKS):
                seen = UNIT0[l] + max(i for i, u in enumerate(us) if u[0] == place) + 1
                stream += [("in", l, ch, hf, (unit_done, seen)) for hf in range(2)]
            for ch in range(2):
                stream += [("o", l, ch, hf, (wo_done, 8 * l + 4 * (ch + 1))) for hf in range(2)]
            if l == 0:
                for kind, j in ORDER:
                    stream += [(kind, l, j, hf, (dd_done if kind == "d" else dg_done, 4 * (j + 1)))
                               for hf in range(2)]
        slot_of, count_of, before = [], [], []
        filled, user, at_slot = [0] * SLOTS, [None] * SLOTS, 0
        for n, item in enumerate(stream):
            if item[:2] == ("in", 1) and stream[n - 1][0] != "in":
                at_slot = 0
            filled[at_slot] += 1
            slot_of.append(at_slot)
            count_of.append(16 * filled[at_slot])
            before.append(user[at_slot])
            user[at_slot] = n
            at_slot = (at_slot + 1) % SLOTS
        halves = {item[:4]: n for n, item in enumerate(stream)}
        assert all(slot_of[n] < FIRST_OVER for n, item in enumerate(stream) if item[0] == "o")

        EXPERT = [(kind, j, hf) for kind, j in ORDER for hf in range(2)]
        PER_E = len(EXPERT)
        FILLS = PER_E // SLOTS
        assert PER_E % SLOTS == 0
        e_slot = [(at_slot + i) % SLOTS for i in range(PER_E)]
        PIECES_E = 2 * PER_E
        e_count = [16 * (filled[e_slot[i]] + i // SLOTS + 1) for i in range(PER_E)]
        e_before = [user[e_slot[i]] for i in range(SLOTS)]
        place_of = {key: i for i, key in enumerate(ORDER)}

        def half_cols(slot):
            return ring[:, slot, :].rearrange("p (k c) -> p k c", k=KT // 2)

        def half_rows(slot):
            return ring[:, slot, :].rearrange("p (i c) -> p i c", i=2)

        TOK_BANKS = (0, 1, 6, 7)
        N_INPUTS = 8
        y_tiles = [0, 1, 2, 10, 11, 16, 17, 18]

        block = ctx.enter_context(nc.Block())

        @block.sync
        def _(sp):
            sp.dma_start(x_tok, x.rearrange("(b p) d -> p b d", p=P)).then_inc(inputs_in, 16)
            sp.dma_start(cst, consts).then_inc(inputs_in, 16)
            sp.dma_start(prm, params).then_inc(inputs_in, 16)

            def fetch(kind, slot, w, j, hf):
                if kind == "d":
                    r0 = CW * j + hf * 2 * P
                    return sp.dma_start(half_rows(slot), w[r0:r0 + 2 * P, :].rearrange("(i p) n -> p i n", p=P))
                lo, hi = CW * j, min(CW * (j + 1), w.shape[1])
                rows = w[hf * 4 * P:(hf + 1) * 4 * P, lo:hi]
                return sp.dma_start(half_cols(slot)[:, :, 0:hi - lo], rows.rearrange("(k p) n -> p k n", p=P))

            for n, (kind, l, j, hf, _) in enumerate(stream):
                slot = slot_of[n]
                if before[n] is not None:
                    sp.wait_ge(*stream[before[n]][4])
                    if stream[before[n]][0] == "in" and kind != "in" and slot >= FIRST_OVER:
                        sp.wait_ge(wo_added, 8 * (l + 1))
                w = {"in": w_in[l], "o": w_o[l], "g": dense_wg[0], "u": dense_wu[0], "d": dense_wd[0]}[kind]
                fetch(kind, slot, w, j, hf).then_inc(ring_in[slot], 16)

            def load_expert(e, i):
                kind, j, hf = EXPERT[i]
                w = {"g": moe_wg, "u": moe_wu, "d": moe_wd}[kind]
                fetch(kind, e_slot[i], w[e], j, hf).then_inc(ring_in[e_slot[i]], 16)

            AHEAD = EXPERT.index(("d", 0, 0)) + 1

            def moe_pass(p):
                base = p * NE * PER_E
                for i in range(SLOTS):
                    if p:
                        sp.wait_ge(lo_ready, 2 * (base + i - SLOTS + 1))
                    else:
                        sp.wait_ge(*stream[e_before[i]][4])
                        if e_slot[i] >= FIRST_OVER:
                            sp.wait_ge(wo_added, 8 * L)
                    load_expert(0, i)
                for i in range(SLOTS, AHEAD):
                    sp.wait_ge(lo_ready, 2 * (base + i - SLOTS + 1))
                    load_expert(0, i)
                with sp.Fori(0, NE - 1) as e:
                    done = e * PIECES_E + 2 * base
                    for i in range(AHEAD, PER_E + AHEAD):
                        sp.wait_ge(lo_ready, done + 2 * (i - SLOTS + 1))
                        load_expert(e + i // PER_E, i % PER_E)
                for i in range(AHEAD, PER_E):
                    sp.wait_ge(lo_ready, 2 * (base + (NE - 1) * PER_E + i - SLOTS + 1))
                    load_expert(NE - 1, i)

            moe_pass(0)
            sp.wait_ge(flag_ready, 1)
            over_full = sp.value_load(flag[0:1, 0:1])
            with sp.If(over_full > 0):
                moe_pass(1)

        @block.gpsimd
        def _(pool):
            pool_steps = [0]

            def then(ins):
                pool_steps[0] += 1
                ins.then_inc(pool_step, 1)
                pool.wait_ge(pool_step, pool_steps[0])

            def convolution(l):
                pool.wait_ge(unit_kept, UNIT0[l] + N_UNITS[l])
                cu, cy, cb = pT[:, 14:16, :], pT[:, 12:14, :], pT[:, 10:12, :]
                then(pool.tensor_tensor(cu, cy, cu, ALU.mult))
                for i in range(2):
                    last = pool.tensor_scalar(cy[:, i, :], cu[:, i, :], param(l, "conv_w", 4 + i), None, ALU.mult)
                then(last)
                for back in (1, 2):
                    for i in range(2):
                        then(pool.tensor_scalar(conv_tmp[:, back:T], cu[:, i, 0:T - back],
                                                param(l, "conv_w", 2 * (2 - back) + i), None, ALU.mult))
                        then(pool.tensor_tensor(cy[:, i, back:T], cy[:, i, back:T], conv_tmp[:, back:T], ALU.add))
                then(pool.tensor_tensor(cy, cy, cb, ALU.mult))
                pool.tensor_tensor(cu, cy, cy, ALU.mult).then_inc(hs_sq, 1)

            pool.wait_ge(inputs_in, 16 * N_INPUTS)
            for l in range(L):
                pool.wait_ge(unit_done, UNIT0[l] + N_UNITS[l])
                if l:
                    pool.wait_ge(x_ffn, 1)
                pool.memset(state, 0.0).then_inc(state_zero, 1)
                for tau in range(2):
                    q = 2 * l + tau
                    if q:
                        pool.wait_ge(p1_done, q)
                    if l and not tau:
                        pool.wait_ge(unit_done, UNIT0[l] + N_UNITS[l])
                    pool.tensor_copy(inv, spread(ident, HEADS)).then_inc(inv_init, 1)
                    pool.tensor_copy(invT, spread(ident, HEADS)).then_inc(inv_init, 1)
                    if not tau:
                        convolution(l)

        @block.tensor
        def _(pe):
            def mm(out_, lhsT, rhs, start=True, stop=True):
                return pe.matmul(out_, lhsT, rhs, start=start, stop=stop)

            pe.wait_ge(inputs_in, 16 * N_INPUTS)
            for i in range(4):
                for k in range(2):
                    for b in range(2):
                        c0 = k * T + b * P
                        last = pe.transpose(bank[i][:, c0:c0 + P], x_tok[:, b, (2 * i + k) * P:(2 * i + k + 1) * P],
                                            ident)
                last.then_inc(x_turned, 1)

            def norm(n):
                pe.wait_ge(sq_ready, n + 1)
                for k in range(KT):
                    last = mm(bank[7][:, 0:T], ones, hT[:, k, :], k == 0, k == KT - 1)
                last.then_inc(ss_ready, 1)

            conv_sq = [pT[:, 14, :], pT[:, 15, :]]

            def head_sum(n, tiles, b):
                for t, sq in enumerate(tiles):
                    last = mm(bank[b][0:SEL_ROWS, 0:T], selin[:, t, :], sq, t == 0, t == len(tiles) - 1)
                last.then_inc(hs_sum, 1)

            def head_spread(n, n_tiles, banks):
                pe.wait_ge(hs_root, n + 1)
                for t in range(n_tiles):
                    last = mm(bank[banks[t // 2]][:, t % 2 * T:t % 2 * T + T], selout[:, t, :],
                              head_rn[0:SEL_ROWS, :])
                last.then_inc(hs_bc, 1)

            def project(l, place, kind, n, first, final, u):
                g = UNIT0[l] + u
                ns = [halves[("in", l, CHUNKS[place], hf)] for hf in range(2)]
                if first:
                    for m in ns:
                        pe.wait_ge(ring_in[slot_of[m]], count_of[m])
                if g >= 4:
                    pe.wait_ge(unit_kept, g - 3)
                b = bank[g % 4]
                for k in range(KT):
                    w = half_cols(slot_of[ns[k // 4]])[:, k % 4, :]
                    if kind == "cm":
                        c0 = n % 4 * P
                        last = mm(b[:, 0:T], w[:, c0:c0 + P], hT[:, k, :], k == 0, k == KT - 1)
                    elif kind == "vres":
                        last = mm(b[0:16, 0:T], vres_wt[:, k, :], hT[:, k, :], k == 0, k == KT - 1)
                    else:
                        h = hT[:, k, n * P:(n + 1) * P]
                        if kind == "va":
                            last = mm(b[:, 0:T], h, w[:, 2 * P:4 * P], k == 0, k == KT - 1)
                        else:
                            last = mm(b[:, 0:P], h, w[:, 0:P], k == 0, k == KT - 1)
                last.then_inc(unit_done, 1)

            def lora_product(kind, l, banks):
                for i in range(NRT):
                    o = bank[banks[i // 2]][:, i % 2 * T:i % 2 * T + T]
                    cols = slice(i * P, (i + 1) * P)
                    if kind == "v":
                        last = mm(o, v2w[0:16, cols], pv[0:16, :])
                    else:
                        r0, r1 = {"w": (0, 32), "a": (32, 64), "g": (64, 128)}[kind]
                        last = mm(o, lora_w[r0:r1, l, cols], lora_in[r0:r1, :])
                last.then_inc(lora_done, 1)

            def recurrence(l, tau):
                q = 2 * l + tau
                ts = slice(tau * P, (tau + 1) * P)
                kT, vT, rT = pT[:, 3:6, :], pT[:, 6:9, :], pT[:, 0:3, :]
                pe.wait_ge(rw_ready, l + 1)
                pe.wait_ge(unit_kept, UNIT0[l] + N_UNITS[l])
                if tau:
                    pe.wait_ge(y_out, q)
                    pe.wait_ge(hs_used, 3 * l + 3)
                for b0, src in zip(TOK_BANKS, (aT, bT, kT, vT)):
                    for i in range(NRT):
                        last = pe.transpose(bank[b0][:, i * P:(i + 1) * P], src[:, i, ts], ident)
                    last.then_inc(tok_done, 1)
                pe.wait_ge(bonus_ready, l + 1)
                for n, (x1, x2, b0) in enumerate(((bT, aT, 4), (aT, bT, 6), (kT, aT, 4), (bT, rT, 6), (kT, rT, 4))):
                    if n == 1:
                        pe.wait_ge(tok_kept_d, 2 * q + 2)
                    if n == 2:
                        pe.wait_ge(gram_kept, 4 * q + 1)
                    if n == 3:
                        pe.wait_ge(inv_ready, 12 * q + 2)
                    if n == 4:
                        pe.wait_ge(gram_kept, 4 * q + 2)
                    for h in range(HEADS):
                        r = slice(h % 2 * HD, h % 2 * HD + HD)
                        last = mm(bank[b0 + h % 2][:, h // 2 * P:(h // 2 + 1) * P], x1[r, h // 2, ts], x2[r, h // 2, ts])
                    last.then_inc(gram_done, 1)
                pe.wait_ge(gram_kept, 4 * q + 3)
                pe.wait_ge(tok_kept_d, 2 * q + 2)
                for h in range(HEADS):
                    last = mm(bank[6][:, h * HD:(h + 1) * HD], gram[1][:, lane(h), :], tok[3][:, h * HD:(h + 1) * HD])
                last.then_inc(lv_done, 1)
                pe.wait_ge(gram_kept, 4 * q + 4)
                pe.wait_ge(tok_kept_a, 2 * q + 2)
                pe.wait_ge(lv_kept, q + 1)
                for lev in range(1, 6):
                    for g in range(2):
                        pe.wait_ge(inv_ready, 12 * q + 2 * (lev - 1) + g + 1)
                        for i in range(3):
                            h = 3 * g + i
                            last = mm(bank[4 + g][:, i * P:(i + 1) * P], gram[0][:, h, :], inv[:, h, :])
                        last.then_inc(lt_done, 1)
                    n = 5 * tau + lev - 1
                    if 1 <= n <= HEADS:
                        times_v(l, n - 1)
                    if n < HEADS:
                        scores(l, n)
                    for g in range(2):
                        pe.wait_ge(lt_kept, 10 * q + 2 * (lev - 1) + g + 1)
                        for i in range(3):
                            h = 3 * g + i
                            last = mm(bank[g][:, i * P:(i + 1) * P], lt[:, h, :], invT[:, h, :])
                        if lev < 5:
                            for i in range(3):
                                h = 3 * g + i
                                last = mm(bank[6 + g][:, i * P:(i + 1) * P], invT[:, h, :], lt[:, h, :])
                        last.then_inc(tlt_done, 1)
                    if n < HEADS:
                        turn_probs(l, n)
                    if n == 9:
                        turn_output(l)
                pe.wait_ge(inv_ready, 12 * q + 12)
                for h in range(HEADS):
                    mm(bank[4][:, h * HD:(h + 1) * HD], invT[:, lane(h), :], lv[:, h * HD:(h + 1) * HD])
                for h in range(HEADS):
                    i = h // 2
                    last = mm(bank[6 + h % 2][:, i * P:(i + 1) * P], tok[0][:, i * P:(i + 1) * P], invT[:, lane(h), :])
                last.then_inc(p1_done, 1)
                if not tau:
                    pe.wait_ge(hs_sq, 2 * l + 2)
                    head_sum(3 * l + 2, conv_sq, 0)
                pe.wait_ge(p1_kept, q + 1)
                pe.wait_ge(ta_kept, q + 1)
                if not tau:
                    pe.wait_ge(state_zero, l + 1)
                for c in range(2):
                    ci = 2 * q + c
                    rows = slice(c * C, (c + 1) * C)
                    if ci:
                        pe.wait_ge(st_ready, ci)
                        pe.wait_ge(yc_kept, ci)
                    for i in range(NRT):
                        last = mm(bank[5][:, i * P:(i + 1) * P], ta_t[:, i, :], state[:, i, :])
                    last.then_inc(u_done, 1)
                    for i in range(NRT):
                        last = mm(bank[6][:, i * P:(i + 1) * P], rT[:, i, ts], state[:, i, :])
                    last.then_inc(yc_done, 1)
                    pe.wait_ge(u_ready, ci + 1)
                    for i in range(NRT):
                        cols = slice(i * P, (i + 1) * P)
                        mm(bank[7][:, cols], tok[1][rows, cols], u_tok[rows, cols], True, False)
                        last = mm(bank[7][:, cols], tok[2][rows, cols], tok[3][rows, cols], False, True)
                    last.then_inc(st_done, 1)
                for h in range(HEADS):
                    cols = slice(h * HD, (h + 1) * HD)
                    mm(bank[4][:, cols], gram[2][:, lane(h), :], u_tok[:, cols], True, False)
                    last = mm(bank[4][:, cols], gram[3][:, lane(h), :], tok[3][:, cols], False, True)
                last.then_inc(y_done, 1)
                if not tau:
                    head_spread(3 * l + 2, 2, (1,))
                pe.wait_ge(yn_ready, q + 1)
                for i in range(NRT):
                    last = pe.transpose(bank[5][:, i * P:(i + 1) * P], y_tok[:, i * P:(i + 1) * P], ident)
                last.then_inc(yt_done, 1)

            def scores(l, h):
                qT, kT = pT[:, 16:19, :], pT[:, 19:22, :]
                a = HEADS * l + h
                r = slice(h % 2 * HD, h % 2 * HD + HD)
                if h == 0:
                    pe.wait_ge(rope_ready, l + 1)
                mm(bank[2][:, 0:P], qT[r, h // 2, 0:P], kT[r, h // 2, 0:P])
                mm(bank[2][:, P:3 * P], qT[r, h // 2, P:T], kT[r, h // 2, :]).then_inc(sc_done, 1)

            def turn_probs(l, h):
                a = HEADS * l + h
                pe.wait_ge(ex_done, a + 1)
                for b in range(3):
                    last = pe.transpose(bank[3][:, b * P:(b + 1) * P], probs[a % 2][:, b * P:(b + 1) * P], ident)
                last.then_inc(tp_done, 1)

            def times_v(l, h):
                a = HEADS * l + h
                pe.wait_ge(tp_kept, a + 1)
                pe.wait_ge(sc_read, a + 1)
                if a:
                    pe.wait_ge(o_ready, a)
                cols = slice(h * HD, (h + 1) * HD)
                mm(bank[2][:, 384:448], probs_t[:, 0:P], v_att[:, 0, cols])
                mm(bank[2][:, 448:512], probs_t[:, P:2 * P], v_att[:, 0, cols], True, False)
                mm(bank[2][:, 448:512], probs_t[:, 2 * P:3 * P], v_att[:, 1, cols], False, True).then_inc(pv_done, 1)

            def turn_output(l):
                pe.wait_ge(on_ready, l + 1)
                for b in range(2):
                    for i in range(NRT):
                        last = pe.transpose(bank[2 + b][:, i * P:(i + 1) * P],
                                            o_tok[:, b, 2 * i:2 * i + 2, :].rearrange("p h d -> p (h d)"), ident)
                last.then_inc(ot_done, 1)

            for l in range(L):
                norm(2 * l)
                pe.wait_ge(h_ready, 2 * l + 1)
                us = units(l)
                for u, unit in enumerate(us):
                    project(l, *unit, u)
                    at = unit[1:3]
                    if at == ("va", 0):
                        pe.wait_ge(qk_sq, l + 1)
                        head_sum(3 * l, [sq_qk[:, i, :] for i in range(6)], 4)
                    if at == ("vb", 0):
                        head_spread(3 * l, 6, (5, 6, 7))
                    if at == ("cm", 8):
                        pe.wait_ge(hs_used, 3 * l + 1)
                        for i in range(6):
                            last = mm(bank[5 + i // 2][:, i % 2 * T:i % 2 * T + T], const("rot"), pT[:, 16 + i, :])
                        last.then_inc(rot_done, 1)
                    if at == ("cm", 0):
                        pe.wait_ge(rope_ready, l + 1)
                        pe.wait_ge(lora_act, l + 1)
                        lora_product("w", l, (4, 5))
                        lora_product("a", l, (6, 7))
                    if at == ("cm", 2):
                        pe.wait_ge(lora_kept, LORA0[l] + 1)
                        lora_product("g", l, (4, 5))
                        if l:
                            pe.wait_ge(lora_kept, LORA0[l] + 2)
                            pe.wait_ge(vres_shifted, l)
                            lora_product("v", l, (6, 7))
                    if at == ("cm", 7):
                        pe.wait_ge(lora_kept, LORA0[l] + LORAS[l])
                        pe.wait_ge(hs_sq, 2 * l + 1)
                        head_sum(3 * l + 1, [tmp1[:, i, :] for i in range(NRT)], 4)
                    if at == ("cm", 13):
                        head_spread(3 * l + 1, 3, (5, 6))
                    if at == ("cm", 14):
                        pe.wait_ge(bonus_in, l + 1)
                        for i in range(NRT):
                            last = mm(bank[(4, 7)[i // 2]][:, i % 2 * T:i % 2 * T + T], const("pair"), tmp2[:, i, :])
                        last.then_inc(bonus_sum, 1)
                recurrence(l, 0)
                recurrence(l, 1)
                pe.wait_ge(att_out, l + 1)
                pe.wait_ge(y_out, 2 * l + 2)
                for m in range(KT):
                    ns = [halves[("o", l, m // 4, hf)] for hf in range(2)]
                    if m % 4 == 0:
                        for n in ns:
                            pe.wait_ge(ring_in[slot_of[n]], count_of[n])
                    if m >= 4:
                        pe.wait_ge(wo_added, 8 * l + m - 3)
                    for k in range(KT):
                        w = half_cols(slot_of[ns[k // 4]])[:, k % 4, m % 4 * P:(m % 4 + 1) * P]
                        last = mm(bank[m % 4][:, 0:T], w,
                                  pT[:, y_tiles[k], :], k == 0, k == KT - 1)
                    last.then_inc(wo_done, 1)
                norm(2 * l + 1)
                pe.wait_ge(h_ready, 2 * l + 2)
                if l == 0:
                    def down(j):
                        for i in range(4):
                            m = 4 * j + i
                            n = halves[("d", 0, j, i // 2)]
                            if i % 2 == 0:
                                pe.wait_ge(ring_in[slot_of[n]], count_of[n])
                            pe.wait_ge(da_ready, m + 1)
                            for dt in range(KT):
                                last = pe.matmul(bank[4 + dt // 2][:, dt % 2 * T:dt % 2 * T + T],
                                                 half_rows(slot_of[n])[:, i % 2, dt * P:(dt + 1) * P],
                                                 dense_act[m % 8], start=(m == 0 and dt % 2 == 0), stop=(m == 27),
                                                 skip_group_check=True)
                            last.then_inc(dd_done, 1)

                    for j in range(NJ):
                        for m in range(4 * j, 4 * j + 4):
                            for which, kind in enumerate("gu"):
                                ns = [halves[(kind, 0, j, hf)] for hf in range(2)]
                                if m % 4 == 0:
                                    for n in ns:
                                        pe.wait_ge(ring_in[slot_of[n]], count_of[n])
                                if m >= 2:
                                    pe.wait_ge(da_ready, m - 1)
                                for k in range(KT):
                                    w = half_cols(slot_of[ns[k // 4]])[:, k % 4, m % 4 * P:(m % 4 + 1) * P]
                                    last = mm(bank[m % 2 + 2 * which][:, 0:T], w, hT[:, k, :], k == 0, k == KT - 1)
                            last.then_inc(dg_done, 1)
                        if j:
                            down(j - 1)
                    down(NJ - 1)

            for b in range(2):
                for k in range(KT):
                    last = mm(bank[0][:, b * NE:(b + 1) * NE], hT[:, k, b * P:(b + 1) * P], router_w[:, k, :],
                              k == 0, k == KT - 1)
            last.then_inc(logit_done, 1)
            mm(bank[1][:, 0:8], const("tri"), router_w[:, 0, :]).then_inc(pc_free, PIECES)
            for f in range(8):
                src, b, hf = (hT, xT)[f // 4], f // 2 % 2, f % 2
                if f >= 4:
                    pe.wait_ge(act_turned, f - 3)
                for i in range(4):
                    last = pe.transpose(bank[4 + f % 4][:, i * P:(i + 1) * P], src[:, 4 * hf + i, b * P:(b + 1) * P],
                                        ident)
                last.then_inc(pe_turned, 1)
            sel = small[:, 0:16]
            pe.wait_ge(route_sel, 1)
            mm(bank[1][:, 0:8], const("tri"), sel[:, 0:8])
            mm(bank[1][:, 8:16], const("tri"), sel[:, 8:16], True, False)
            mm(bank[1][:, 8:16], ones, sel[:, 0:8], False, True)
            mm(bank[1][:, 16:24], ones, sel[:, 0:8], True, False)
            mm(bank[1][:, 16:24], ones, sel[:, 8:16], False, True).then_inc(rank_done, 1)

            def moe_pass(p):
                pe.wait_ge(oh_ready, p + 1)
                if p == 0:
                    pe.wait_ge(act_turned, 8)
                for f in range(4):
                    if f >= 2:
                        pe.wait_ge(cb_kept, 4 * p + f - 1)
                    for i in range(2):
                        for b in range(2):
                            c0 = i * T + b * P
                            last = pe.transpose(bank[6 + f % 2][:, c0:c0 + P], gated[:, b, 2 * f + i, :], ident)
                    last.then_inc(cb_done, 1)
                pe.wait_ge(cb_kept, 4 * p + 4)

                def gather(e, at1):
                    for f in range(2):
                        for i in range(4):
                            k = 4 * f + i
                            for b in range(2):
                                last_ = mm(bank[1 + 2 * f][:, i * P:(i + 1) * P], h_tok[:, b, k * P:(k + 1) * P],
                                           onehot[:, b, e, :], b == 0, b == 1)
                        last_.then_inc(ga_done, 1)

                def three(out_, a_hi, a_lo, b_hi, b_lo, first, final):
                    mm(out_, a_hi, b_hi, first, False)
                    mm(out_, a_hi, b_lo, False, False)
                    return mm(out_, a_lo, b_hi, False, final)

                def column_chunk(kind, j, at1):
                    if j >= 2:
                        pe.wait_ge(ac_ready, at1 * NJ + (j - 1))
                    b = bank[(0 if kind == "g" else 2) + j % 2]
                    for q in range(4):
                        pe.wait_ge(lo_ready, at1 * PIECES_E + (4 * place_of[(kind, j)] + q + 1))
                        for i in range(2):
                            k = 2 * q + i
                            ks, cs = slice(k * P, (k + 1) * P), slice(i * CW, (i + 1) * CW)
                            last_ = three(b[:, :], xg_hi[:, ks], xg_lo[:, ks], w_hi[:, q, cs], w_lo[:, q, cs],
                                          k == 0, k == KT - 1)
                        last_.then_inc(pc_free, 1)

                def turn(j, at1):
                    pe.wait_ge(ac_ready, at1 * NJ + (j + 1))
                    if j:
                        pe.wait_ge(at_low, at1 * NJ + j)
                    else:
                        pe.wait_ge(cbe_ready, at1 + 1)
                    for i in range(4):
                        last_ = pe.transpose(bank[6][:, i * P:(i + 1) * P], act_b[j % 2][:, i * P:(i + 1) * P],
                                             ident)
                    last_.then_inc(at_done, 1)

                def down(j, at1):
                    pe.wait_ge(at_low, at1 * NJ + (j + 1))
                    for q in range(4):
                        pe.wait_ge(lo_ready, at1 * PIECES_E + (4 * place_of[("d", j)] + q + 1))
                        for hf in range(2):
                            ks, cs = slice(q * P, (q + 1) * P), slice(hf * CW, (hf + 1) * CW)
                            last_ = three(bank[4 + hf][:, :], at_hi[:, j % 2, ks], at_lo[:, j % 2, ks],
                                          w_hi[:, q, cs], w_lo[:, q, cs], j == 0 and q == 0, j == NJ - 1 and q == 3)
                        last_.then_inc(pc_free, 1)

                def scatter(at1):
                    pe.wait_ge(yg_kept, at1 * 2 + 2)
                    pe.wait_ge(cbe_ready, at1 + 1)
                    for f in range(4):
                        b, hf = f // 2, f % 2
                        mm(bank[(6, 7, 4, 5)[f]][:, :], combine_e[:, b * P:(b + 1) * P],
                           yg[:, hf * 512:(hf + 1) * 512]).then_inc(sct_done, 1)

                def expert(e, at1, last_one):
                    for j in range(1, NJ):
                        column_chunk("g", j, at1)
                        turn(j - 1, at1)
                        column_chunk("u", j, at1)
                        down(j - 1, at1)
                    turn(NJ - 1, at1)
                    if not last_one:
                        gather(e + 1, at1 + 1)
                    down(NJ - 1, at1)
                    if not last_one:
                        pe.wait_ge(ga_low, at1 * 2 + 4)
                        column_chunk("g", 0, at1 + 1)
                    scatter(at1)
                    if not last_one:
                        column_chunk("u", 0, at1 + 1)

                first = p * NE
                gather(0, first)
                pe.wait_ge(ga_low, first * 2 + 2)
                column_chunk("g", 0, first)
                column_chunk("u", 0, first)
                with pe.Fori(0, NE - 1) as e:
                    expert(e, e + first, False)
                expert(NE - 1, first + NE - 1, True)

            moe_pass(0)
            pe.wait_ge(flag_ready, 1)
            over_full = pe.value_load(flag[0:1, 0:1])
            with pe.If(over_full > 0):
                moe_pass(1)

        @block.scalar
        def _(act):
            steps = [0]

            def then(ins):
                steps[0] += 1
                ins.then_inc(act_step, 1)
                act.wait_ge(act_step, steps[0])

            def copy(o, i, **kw):
                return act.activation(o, i, ACT.Copy, **kw)

            act.dma_start(mask_in, masks).then_inc(inputs_in, 16)
            act.dma_start(lora_w, lora.rearrange("l p n -> p l n")).then_inc(inputs_in, 16)
            act.dma_start(v2w[0:16, :], vres_v2).then_inc(inputs_in, 16)
            act.dma_start(vres_wt, vres_w.rearrange("(k p) n -> p k n", p=P)).then_inc(inputs_in, 16)
            act.dma_start(router_w, router.rearrange("(k p) n -> p k n", p=P)).then_inc(inputs_in, 16)
            for i in range(4):
                act.wait_ge(x_turned, i + 1)
                copy(xT[:, 2 * i:2 * i + 2, :].rearrange("p k t -> p (k t)"), bank[i][:, :]).then_inc(x_kept, 1)

            def norm(n, ready):
                act.wait_ge(*ready)
                act.activation(hT, xT, ACT.Square).then_inc(sq_ready, 1)
                act.wait_ge(ms_ready, n + 1)
                act.activation(rn, rn, ACT.Sqrt).then_inc(rn_ready, 1)

            def root(n):
                act.wait_ge(hs_rec, n + 1)
                act.activation(head_rn[0:SEL_ROWS, :], head_rn[0:SEL_ROWS, :], ACT.Sqrt).then_inc(hs_root, 1)

            def keep_unit(l, u, kind, n):
                g = UNIT0[l] + u
                act.wait_ge(unit_done, g + 1)
                b = bank[g % 4]
                if kind == "cm":
                    ins = copy(pT[:, n, :], b[:, 0:T])
                elif kind == "vres":
                    ins = copy(pv[0:16, :], b[0:16, 0:T])
                elif kind == "va":
                    ins = copy(v_att[:, n, 0:2 * P], b[:, 0:2 * P])
                else:
                    ins = copy(v_att[:, n, 2 * P:3 * P], b[:, 0:P])
                ins.then_inc(unit_kept, 1)

            def keep_lora(l, n, o, banks, func, bias):
                act.wait_ge(lora_done, LORA0[l] + n + 1)
                for i in range(NRT):
                    src = bank[banks[i // 2]][:, i % 2 * T:i % 2 * T + T]
                    if bias:
                        last = act.activation(o[:, i, :], src, func, bias=param(l, bias, i))
                    else:
                        last = copy(o[:, i, :], src)
                last.then_inc(lora_kept, 1)

            def recurrence(l, tau):
                q = 2 * l + tau
                for n in range(2):
                    act.wait_ge(tok_done, 4 * q + n + 1)
                    copy(tok[n], bank[TOK_BANKS[n]][:, 0:RW]).then_inc(tok_kept_a, 1)
                act.wait_ge(lv_done, q + 1)
                copy(lv, bank[6][:, 0:RW]).then_inc(lv_kept, 1)
                for lev in range(1, 6):
                    for g in range(2):
                        act.wait_ge(lt_done, 10 * q + 2 * (lev - 1) + g + 1)
                        copy(lt[:, 3 * g:3 * g + 3, :].rearrange("p h t -> p (h t)"), bank[4 + g][:, 0:3 * P]).then_inc(
                            lt_kept, 1)
                    n = 5 * tau + lev - 1
                    if n < HEADS:
                        exponentials(l, n)
                    if n == 8:
                        act.wait_ge(on_rec, l + 1)
                        act.activation(small[:, 96:108], small[:, 96:108], ACT.Sqrt).then_inc(on_root, 1)
                act.wait_ge(p1_done, q + 1)
                copy(p1, bank[4][:, 0:RW])
                copy(ta_t[0:HD, :, :].rearrange("p i t -> p (i t)"), bank[6][0:HD, 0:RW]).then_inc(p1_kept, 1)
                for c in range(2):
                    rows = slice(c * C, (c + 1) * C)
                    act.wait_ge(yc_done, 2 * q + c + 1)
                    copy(y_cross[rows, :], bank[6][rows, 0:RW]).then_inc(yc_kept, 1)
                if not tau:
                    root(3 * l + 2)
                act.wait_ge(gn_rec, q + 1)
                act.activation(small[:, 64:70], small[:, 64:70], ACT.Sqrt).then_inc(gn_root, 1)

            def exponentials(l, h):
                a = HEADS * l + h
                act.wait_ge(mx_ready, a + 1)
                for b, cols in enumerate((slice(0, P), slice(P, 3 * P))):
                    pr = probs[a % 2][:, cols]
                    at_ = 2 * (a % 2) + b
                    last = act.activation(pr, pr, ACT.Exp, bias=small[:, 80 + at_:81 + at_],
                                          accum_out=small[:, 84 + at_:85 + at_])
                last.then_inc(ex_done, 1)
                act.wait_ge(tp_done, a + 1)
                copy(probs_t, bank[3][:, 0:3 * P]).then_inc(tp_kept, 1)

            act.wait_ge(inputs_in, 16 * N_INPUTS)
            for l in range(L):
                norm(2 * l, (x_ffn, 1) if l else (x_kept, 4))
                us = units(l)
                for u, (_, kind, n, _, _) in enumerate(us):
                    keep_unit(l, u, kind, n)
                    if (kind, n) == ("cm", 21):
                        act.wait_ge(unit_kept, kept(l, "cm", 21))
                        act.activation(sq_qk, pT[:, 16:22, :], ACT.Square).then_inc(qk_sq, 1)
                    if (kind, n) == ("va", 1):
                        root(3 * l)
                    if (kind, n) == ("cm", 11):
                        act.wait_ge(lora_ready, l + 1)
                        act.activation(lora_in[0:32, :], lora_in[0:32, :], ACT.Tanh)
                        act.activation(lora_in[64:128, :], lora_in[64:128, :], ACT.Sigmoid).then_inc(lora_act, 1)
                    if (kind, n) == ("cm", 1):
                        keep_lora(l, 0, sig_w, (4, 5), ACT.Sigmoid, "w0")
                        keep_lora(l, 1, a_gate, (6, 7), ACT.Sigmoid, "a0")
                    if (kind, n) == ("cm", 3):
                        keep_lora(l, 2, g_gate, (4, 5), ACT.Copy, None)
                        if l:
                            keep_lora(l, 3, bonus, (6, 7), ACT.Sigmoid, "vres_v0")
                    if (kind, n) == ("cm", 5):
                        act.wait_ge(cs_ready, l + 1)
                        then(act.activation(inv_w.rearrange("p i (c t) -> p i c t", c=NC), w65[:, :, :, 1:C + 1],
                                            ACT.Exp, scale=DECAY))
                        act.activation(w65, w65, ACT.Exp, scale=-DECAY).then_inc(w_ready, 1)
                    if (kind, n) == ("cm", 12):
                        root(3 * l + 1)
                recurrence(l, 0)
                recurrence(l, 1)
                norm(2 * l + 1, (wo_added, 8 * (l + 1)))
                if l == 0:
                    for m in range(F // P):
                        act.wait_ge(dg_done, m + 1)
                        if m >= 2:
                            act.wait_ge(da_ready, m - 1)
                        act.activation(dense_sil[m % 2], bank[m % 2][:, 0:T], ACT.Silu).then_inc(ds_done, 1)

            for f in range(8):
                dst, b, hf = (h_tok, x_tok)[f // 4], f // 2 % 2, f % 2
                act.wait_ge(pe_turned, f + 1)
                copy(dst[:, b, 512 * hf:512 * (hf + 1)], bank[4 + f % 4][:, :]).then_inc(act_turned, 1)
            act.wait_ge(route_act, 1)
            act.activation(top_gap, top_gap, ACT.Exp).then_inc(route_exp, 1)

            def moe_pass(p):
                for f in range(4):
                    act.wait_ge(cb_done, 4 * p + f + 1)
                    copy(combine[:, 2 * f:2 * f + 2, :].rearrange("p e t -> p (e t)"), bank[6 + f % 2][:, :]).then_inc(
                        cb_kept, 1)

                def split(kind, j, at1):
                    for q in range(4):
                        c = 4 * place_of[(kind, j)] + q
                        h = c // 2
                        if q % 2 == 0:
                            act.wait_ge(ring_in[e_slot[h]], at1 * (16 * FILLS) + e_count[h])
                        act.wait_ge(pc_free, at1 * PIECES_E + (c + 1))
                        raw = ring[:, e_slot[h], c % 2 * PIECE:(c % 2 + 1) * PIECE]
                        copy(w_hi[:, q, :], raw).then_inc(hi_ready, 1)

                def gathered(at1):
                    for f in range(2):
                        act.wait_ge(ga_done, at1 * 2 + (f + 1))
                        copy(xg_hi[:, f * CW:(f + 1) * CW], bank[1 + 2 * f][:, :]).then_inc(ga_kept, 1)

                def silu(j, at1):
                    act.wait_ge(pc_free, at1 * PIECES_E + (4 * (place_of[("g", j)] + 1) + PIECES))
                    if j >= 2:
                        act.wait_ge(ac_ready, at1 * NJ + (j - 1))
                    act.activation(sil_b[j % 2], bank[j % 2][:, :], ACT.Silu).then_inc(sl_done, 1)

                def turned(j, at1):
                    act.wait_ge(at_done, at1 * NJ + (j + 1))
                    copy(at_hi[:, j % 2, :], bank[6][:, :]).then_inc(at_kept, 1)

                def expert(e, at1, last_one):
                    for j in range(1, NJ):
                        split("g", j, at1)
                        split("u", j, at1)
                        turned(j - 1, at1)
                        silu(j, at1)
                        split("d", j - 1, at1)
                    split("d", NJ - 1, at1)
                    turned(NJ - 1, at1)
                    if not last_one:
                        gathered(at1 + 1)
                        split("g", 0, at1 + 1)
                    act.wait_ge(pc_free, at1 * PIECES_E + (PIECES_E + PIECES))
                    for hf in range(2):
                        copy(yg[:, hf * 512:(hf + 1) * 512], bank[4 + hf][:, :]).then_inc(yg_kept, 1)
                    if not last_one:
                        split("u", 0, at1 + 1)
                        silu(0, at1 + 1)

                first = p * NE
                gathered(first)
                split("g", 0, first)
                split("u", 0, first)
                silu(0, first)
                with act.Fori(0, NE - 1) as e:
                    expert(e, e + first, False)
                expert(NE - 1, first + NE - 1, True)

            moe_pass(0)
            act.wait_ge(flag_ready, 1)
            over_full = act.value_load(flag[0:1, 0:1])
            with act.If(over_full > 0):
                moe_pass(1)
            act.wait_ge(moe_done, 1)
            act.dma_start(out.rearrange("(b p) d -> p b d", p=P), x_tok).then_inc(out_done, 16)
            act.wait_ge(out_done, 16)

        @block.vector
        def _(dve):
            steps = [0]

            def then(ins):
                steps[0] += 1
                ins.then_inc(dve_step, 1)
                dve.wait_ge(dve_step, steps[0])

            TT = dve.tensor_tensor
            TS = dve.tensor_scalar
            STT = dve.scalar_tensor_tensor

            def norm(n, l, gain):
                dve.wait_ge(ss_ready, n + 1)
                then(TS(rn, bank[7][:, 0:T], 1.0 / D, NORM_EPS, ALU.mult, ALU.add))
                dve.reciprocal(rn, rn).then_inc(ms_ready, 1)
                dve.wait_ge(rn_ready, n + 1)
                for k in range(KT):
                    last = STT(hT[:, k, :], xT[:, k, :], param(l, gain, k), rn, ALU.mult, ALU.mult)
                last.then_inc(h_ready, 1)
                dve.wait_ge(h_ready, n + 1)

            def shift(l, p_, mu, t_, o_=None, rows=P):
                n = p_.shape[1]
                t_ = t_[:, 0:n, :]
                then(TS(t_[0:rows, :, 0:1], p_[0:rows, :, 0:1], -1.0, None, ALU.mult))
                then(TT(t_[0:rows, :, 1:T], p_[0:rows, :, 0:T - 1], p_[0:rows, :, 1:T], ALU.subtract))
                for i in range(n):
                    o = p_[0:rows, i, :] if o_ is None else o_
                    ins = STT(o, t_[0:rows, i, :], mu(i)[0:rows, :], p_[0:rows, i, :], ALU.mult, ALU.add)
                return ins

            def head_factor(n, b, first, second, ops):
                dve.wait_ge(hs_sum, n + 1)
                then(TS(head_rn[0:SEL_ROWS, :], bank[b][0:SEL_ROWS, 0:T], first, second, *ops))
                dve.reciprocal(head_rn[0:SEL_ROWS, :], head_rn[0:SEL_ROWS, :]).then_inc(hs_rec, 1)

            def recurrence(l, tau):
                q = 2 * l + tau
                for n in (2, 3):
                    dve.wait_ge(tok_done, 4 * q + n + 1)
                    TS(tok[n], bank[TOK_BANKS[n]][:, 0:RW], 1.0, None, ALU.mult).then_inc(tok_kept_d, 1)
                strict = spread(const("strict"), 3)
                incl = spread(const("incl"), 3)

                def as3(b):
                    return bank[b][:, 0:3 * P].rearrange("p (i t) -> p i t", i=3)

                def keep_gram(n, g_, mask, b0):
                    dve.wait_ge(gram_done, 5 * q + n + 1)
                    for g in range(2):
                        last = TT(gram[g_][:, 3 * g:3 * g + 3, :], as3(b0 + g), mask, ALU.mult)
                    last.then_inc(gram_kept, 1)

                dve.wait_ge(inv_init, 2 * q + 2)
                dve.wait_ge(gram_done, 5 * q + 1)
                for g in range(2):
                    then(dve.copy_predicated(invT[:, 3 * g:3 * g + 3, :], spread(lmask[:, 1, 0, :], 3), as3(4 + g)))
                keep_gram(0, 0, strict, 4)
                dve.wait_ge(gram_done, 5 * q + 2)
                for g in range(2):
                    dve.copy_predicated(inv[:, 3 * g:3 * g + 3, :], spread(lmask[:, 0, 0, :], 3), as3(6 + g)).then_inc(
                        inv_ready, 1)
                keep_gram(2, 1, strict, 4)
                keep_gram(3, 2, incl, 6)
                keep_gram(4, 3, incl, 4)
                for lev in range(1, 6):
                    n = 5 * tau + lev - 1
                    if n < HEADS:
                        largest_score(l, n)
                    for g in range(2):
                        hs = slice(3 * g, 3 * g + 3)
                        dve.wait_ge(tlt_done, 10 * q + 2 * (lev - 1) + g + 1)
                        last = dve.copy_predicated(invT[:, hs, :], spread(lmask[:, 1, lev, :], 3), as3(g))
                        if lev < 5:
                            then(last)
                            last = dve.copy_predicated(inv[:, hs, :], spread(lmask[:, 0, lev, :], 3), as3(6 + g))
                        last.then_inc(inv_ready, 1)
                    if 1 <= n <= HEADS:
                        keep_output(l, n - 1)
                    if n == HEADS + 1:
                        output_squares(l)
                    if n == HEADS + 2:
                        dve.wait_ge(on_root, l + 1)
                        TT(o12, o12, stretch(out_ss, HD), ALU.mult).then_inc(on_ready, 1)
                dve.wait_ge(p1_done, q + 1)
                TS(ta_t[HD:P, :, :].rearrange("p i t -> p (i t)"), bank[7][HD:P, 0:RW], 1.0, None, ALU.mult).then_inc(
                    ta_kept, 1)
                dve.wait_ge(p1_kept, q + 1)
                for c in range(2):
                    ci = 2 * q + c
                    rows = slice(c * C, (c + 1) * C)
                    chunk = 2 * tau + c
                    then(TT(end_w, spread(const("pair"), NRT),
                            w65[:, :, chunk, C:C + 1].to_broadcast([P, NRT, P]), ALU.mult))
                    dve.wait_ge(u_done, ci + 1)
                    TT(u_tok[rows, :], bank[5][rows, 0:RW], p1[rows, :], ALU.add).then_inc(u_ready, 1)
                    dve.wait_ge(st_done, ci + 1)
                    then(TT(state_tmp, bank[7][:, 0:RW].rearrange("p (i v) -> p i v", i=NRT), state, ALU.add))
                    TT(state, state_tmp, end_w, ALU.mult).then_inc(st_ready, 1)
                    dve.wait_ge(st_ready, ci + 1)
                if tau:
                    dve.wait_ge(ot_done, l + 1)
                    for b in range(2):
                        for i in range(NRT):
                            last = TS(pT[:, 16 + i, b * P:(b + 1) * P], bank[2 + b][:, i * P:(i + 1) * P],
                                      param(l, "out_g", i), None, ALU.mult)
                    last.then_inc(att_out, 1)
                else:
                    head_factor(3 * l + 2, 0, 1.0 / HD, NORM_EPS, (ALU.mult, ALU.add))
                y3 = y_tok.rearrange("p (h d) -> p h d", h=HEADS)
                dve.wait_ge(y_done, q + 1)
                dve.wait_ge(yc_kept, 2 * q + 2)
                then(TT(y_tok, bank[4][:, 0:RW], y_cross, ALU.add))
                mean, var = small[:, 70:76], small[:, 64:70]
                then(dve.tensor_reduce(mean, y3, AX.X, ALU.add))
                then(TS(mean, mean, 1.0 / HD, None, ALU.mult))
                then(TT(y3, y3, stretch(mean, HD), ALU.subtract))
                sq3 = y_cross.rearrange("p (h d) -> p h d", h=HEADS)
                then(TT(sq3, y3, y3, ALU.mult))
                then(dve.tensor_reduce(var, sq3, AX.X, ALU.add))
                then(TS(var, var, 1.0 / HD, GN_EPS, ALU.mult, ALU.add))
                dve.reciprocal(var, var).then_inc(gn_rec, 1)
                if not tau:
                    dve.wait_ge(hs_bc, 3 * l + 3)
                    for i in range(2):
                        last = STT(pT[:, 10 + i, :], pT[:, 12 + i, :], param(l, "conv_g", i),
                                   bank[1][:, i * T:(i + 1) * T], ALU.mult, ALU.mult)
                    last.then_inc(hs_used, 1)
                dve.wait_ge(gn_root, q + 1)
                TT(y3, y3, stretch(var, HD), ALU.mult).then_inc(yn_ready, 1)
                dve.wait_ge(yt_done, q + 1)
                ts = slice(tau * P, (tau + 1) * P)
                for i in range(NRT):
                    last = TS(pT[:, i, ts], bank[5][:, i * P:(i + 1) * P], param(l, "ln_w", i), param(l, "ln_b", i),
                              ALU.mult, ALU.add)
                then(last)
                then(TT(pT[:, 0:3, ts], pT[:, 0:3, ts], bonus[:, :, ts], ALU.add))
                TT(pT[:, 0:3, ts], pT[:, 0:3, ts], g_gate[:, :, ts], ALU.mult).then_inc(y_out, 1)
                dve.wait_ge(y_out, q + 1)

            def largest_score(l, h):
                a = HEADS * l + h
                pr = probs[a % 2]
                nmax = small[:, 80 + 2 * (a % 2):82 + 2 * (a % 2)]
                dve.wait_ge(sc_done, a + 1)
                if a >= 2:
                    dve.wait_ge(tp_done, a - 1)
                STT(pr, bank[2][:, 0:3 * P], HD ** -0.5, const("bias"), ALU.mult, ALU.add).then_inc(sc_read, 1)
                dve.wait_ge(sc_read, a + 1)
                dve.tensor_reduce(nmax[:, 0:1], pr[:, 0:P], AX.X, ALU.max)
                then(dve.tensor_reduce(nmax[:, 1:2], pr[:, P:3 * P], AX.X, ALU.max))
                TS(nmax, nmax, -1.0, None, ALU.mult).then_inc(mx_ready, 1)

            def keep_output(l, h):
                a = HEADS * l + h
                at_ = 2 * (a % 2)
                dve.wait_ge(ex_done, a + 1)
                then(dve.reciprocal(small[:, 88 + at_:90 + at_], small[:, 84 + at_:86 + at_]))
                dve.wait_ge(pv_done, a + 1)
                for b in range(2):
                    last = TS(o_tok[:, b, h, :], bank[2][:, 384 + b * HD:384 + (b + 1) * HD],
                              small[:, 88 + at_ + b:89 + at_ + b], None, ALU.mult)
                last.then_inc(o_ready, 1)
                dve.wait_ge(o_ready, a + 1)

            out_ss = small[:, 96:108]
            o12 = o_tok.rearrange("p b h d -> p (b h) d")

            def output_squares(l):
                s12 = o_sq.rearrange("p b h d -> p (b h) d")
                then(TT(s12, o12, o12, ALU.mult))
                then(dve.tensor_reduce(out_ss, s12, AX.X, ALU.add))
                then(TS(out_ss, out_ss, 1.0 / HD, NORM_EPS, ALU.mult, ALU.add))
                dve.reciprocal(out_ss, out_ss).then_inc(on_rec, 1)

            dve.wait_ge(inputs_in, 16 * N_INPUTS)
            then(dve.tensor_copy(mask8[:, :], mask_in))
            for l in range(L):
                norm(2 * l, l, "mix_norm")
                rT, kT, vT = pT[:, 0:3, :], pT[:, 3:6, :], pT[:, 6:9, :]
                head_factor(3 * l, 4, 1.0 / HD, NORM_EPS, (ALU.mult, ALU.add))
                dve.wait_ge(hs_bc, 3 * l + 1)
                for i in range(6):
                    last = STT(pT[:, 16 + i, :], pT[:, 16 + i, :], param(l, "q_g" if i < 3 else "k_g"),
                               bank[5 + i // 2][:, i % 2 * T:i % 2 * T + T], ALU.mult, ALU.mult)
                last.then_inc(hs_used, 1)
                dve.wait_ge(rot_done, l + 1)
                for i in range(3):
                    TT(sq_qk[:, 2 * i:2 * i + 2, :], bank[5 + i][:, :].rearrange("p (i t) -> p i t", i=2),
                       spread(const("sin"), 2), ALU.mult)
                qk = pT[:, 16:22, :]
                then(TT(qk, qk, spread(const("cos"), 6), ALU.mult))
                TT(qk, qk, sq_qk, ALU.add).then_inc(rope_ready, 1)
                dve.wait_ge(unit_kept, kept(l, "cm", 9))
                shift(l, pT[:, 9:10, :], lambda i: param(l, "mu", 9), tmp1, lora_in).then_inc(lora_ready, 1)
                dve.wait_ge(lora_ready, l + 1)
                if l:
                    dve.wait_ge(unit_kept, kept(l, "vres", 0))
                    pv3 = pv.rearrange("p (a t) -> p a t", a=1)
                    shift(l, pv3, lambda i: param(l, "vres_mu"), tmp1, None, 16).then_inc(vres_shifted, 1)
                    dve.wait_ge(vres_shifted, l)
                dve.wait_ge(unit_kept, kept(l, "cm", 2))
                then(shift(l, rT, lambda i: param(l, "mu", i), tmp1))
                dve.memset(w65[:, :, :, 0:1], 0.0)
                dve.wait_ge(lora_kept, LORA0[l] + 1)
                for i in range(NRT):
                    for c in range(NC):
                        last = dve.tensor_tensor_scan(w65[:, i, c, 1:C + 1], const("ones")[:, 0:C],
                                                      sig_w[:, i, c * C:(c + 1) * C], 0.0, ALU.mult, ALU.add)
                last.then_inc(cs_ready, 1)
                dve.wait_ge(unit_kept, kept(l, "cm", 5))
                then(shift(l, kT, lambda i: param(l, "mu", 3 + i), tmp1))
                for i in range(NRT):
                    last = TS(kk[:, i, :], kT[:, i, :], param(l, "k_k", i), None, ALU.mult)
                then(last)
                TT(tmp1, kk, kk, ALU.mult).then_inc(hs_sq, 1)
                dve.wait_ge(lora_kept, LORA0[l] + 2)
                for i in range(NRT):
                    last = TS(tmp2[:, i, :], a_gate[:, i, :], 1.0, param(l, "k_a", i), ALU.subtract, ALU.mult)
                then(last)
                for i in range(NRT):
                    last = STT(kT[:, i, :], tmp2[:, i, :], 1.0, kT[:, i, :], ALU.add, ALU.mult)
                then(last)
                for i in range(NRT):
                    last = STT(tmp2[:, i, :], rT[:, i, :], param(l, "r_k", i), kT[:, i, :], ALU.mult, ALU.mult)
                last.then_inc(bonus_in, 1)
                dve.wait_ge(bonus_in, l + 1)
                dve.wait_ge(w_ready, l + 1)
                TT(kT, kT, inv_w, ALU.mult)
                TT(rT.rearrange("p i (c t) -> p i c t", c=NC), rT.rearrange("p i (c t) -> p i c t", c=NC),
                   w65[:, :, :, 1:C + 1], ALU.mult)
                dve.wait_ge(hs_sum, 3 * l + 2)
                then(TS(head_rn[0:SEL_ROWS, :], bank[4][0:SEL_ROWS, 0:T], 1e-24, None, ALU.max))
                dve.reciprocal(head_rn[0:SEL_ROWS, :], head_rn[0:SEL_ROWS, :]).then_inc(hs_rec, 1)
                dve.wait_ge(unit_kept, kept(l, "cm", 7))
                then(shift(l, vT, lambda i: param(l, "mu", 6 + i), tmp1))
                if l == 0:
                    then(TS(v_first, vT, 1.0, None, ALU.mult))
                else:
                    dve.wait_ge(lora_kept, LORA0[l] + 4)
                    then(TT(tmp1, v_first, vT, ALU.subtract))
                    then(TT(tmp1, tmp1, bonus, ALU.mult))
                    then(TT(vT, vT, tmp1, ALU.add))
                dve.wait_ge(hs_bc, 3 * l + 2)
                TT(kk[:, 0:2, :], kk[:, 0:2, :], bank[5][:, :].rearrange("p (i t) -> p i t", i=2), ALU.mult)
                TT(kk[:, 2, :], kk[:, 2, :], bank[6][:, 0:T], ALU.mult).then_inc(hs_used, 1)
                dve.wait_ge(hs_used, 3 * l + 2)
                then(TT(a_gate, kk, a_gate, ALU.mult))
                dve.wait_ge(bonus_sum, l + 1)
                TT(bonus[:, 0:2, :], bank[4][:, :].rearrange("p (i t) -> p i t", i=2), vT[:, 0:2, :], ALU.mult)
                TT(bonus[:, 2, :], bank[7][:, 0:T], vT[:, 2, :], ALU.mult).then_inc(bonus_ready, 1)
                dve.wait_ge(unit_done, UNIT0[l] + N_UNITS[l])
                for i in range(NRT):
                    STT(aT[:, i, :].rearrange("p (c t) -> p c t", c=NC),
                        kk[:, i, :].rearrange("p (c t) -> p c t", c=NC), -1.0, w65[:, i, :, 0:C],
                        ALU.mult, ALU.mult)
                TT(bT, a_gate, inv_w, ALU.mult).then_inc(rw_ready, 1)
                recurrence(l, 0)
                recurrence(l, 1)
                for m in range(KT):
                    dve.wait_ge(wo_done, 8 * l + m + 1)
                    TT(xT[:, m, :], xT[:, m, :], bank[m % 4][:, 0:T], ALU.add).then_inc(wo_added, 1)
                dve.wait_ge(wo_added, 8 * l + 8)
                norm(2 * l + 1, l, "ffn_norm")
                if l == 0:
                    for m in range(F // P):
                        dve.wait_ge(ds_done, m + 1)
                        dve.wait_ge(dg_done, m + 1)
                        if m >= 8:
                            dve.wait_ge(dd_done, m - 7)
                        TT(dense_act[m % 8], dense_sil[m % 2], bank[2 + m % 2][:, 0:T], ALU.mult).then_inc(da_ready, 1)
                    dve.wait_ge(dd_done, F // P)
                    for i in range(4):
                        last = TT(xT[:, 2 * i:2 * i + 2, :], xT[:, 2 * i:2 * i + 2, :],
                                  bank[4 + i][:, :].rearrange("p (k t) -> p k t", k=2), ALU.add)
                    last.then_inc(x_ffn, 1)
                    dve.wait_ge(x_ffn, 1)

            def cols(at, n=16):
                return small[:, at:at + n]

            def per(ap):
                return ap.rearrange("p (b e) -> p b e", b=2)

            sel, logits, first, second, cand, gates = (cols(16 * n) for n in range(6))
            top1, top2, at_, g1, g2 = (cols(128 + 2 * n, 2) for n in range(5))
            rank, cmax = cols(144), cols(162, 1)
            e2 = top_gap
            iota8 = spread(const("iota")[:, 0:NE], 2)
            dve.wait_ge(logit_done, 1)
            then(TS(logits, bank[0][:, 0:16], 1.0, None, ALU.mult))

            def largest(value, hot):
                then(dve.tensor_reduce(value, per(logits), AX.X, ALU.max))
                then(TT(per(cand), per(logits), stretch(value, NE), ALU.not_equal))
                then(STT(per(cand), per(cand), float(NE), iota8, ALU.mult, ALU.add))
                then(dve.tensor_reduce(at_, per(cand), AX.X, ALU.min))
                then(TT(per(hot), iota8, stretch(at_, NE), ALU.is_equal))

            largest(top1, first)
            then(STT(logits, first, -3e38, logits, ALU.mult, ALU.add))
            largest(top2, second)
            TT(sel, first, second, ALU.add).then_inc(route_sel, 1)
            TT(e2, top2, top1, ALU.subtract).then_inc(route_act, 1)
            dve.wait_ge(route_exp, 1)
            then(TS(g1, e2, 1.0, None, ALU.add))
            then(dve.reciprocal(g1, g1))
            then(TT(g2, e2, g1, ALU.mult))
            then(TT(per(gates), per(first), stretch(g1, NE), ALU.mult))
            then(TT(per(cand), per(second), stretch(g2, NE), ALU.mult))
            then(TT(gates, gates, cand, ALU.add))
            dve.wait_ge(rank_done, 1)
            TS(rank, bank[1][:, 0:16], 1.0, None, ALU.mult)
            then(dve.tensor_reduce(cmax, bank[1][:, 16:24], AX.X, ALU.max))
            TS(flag[:, :], cmax, float(P), None, ALU.is_gt).then_inc(flag_ready, 1)
            dve.wait_ge(flag_ready, 1)

            def moe_pass(p):
                if p:
                    then(TS(rank, rank, -float(P), None, ALU.add))
                for b in range(2):
                    for e in range(NE):
                        c = b * NE + e
                        last = TS(onehot[:, b, e, :], const("iota"), rank[:, c:c + 1], sel[:, c:c + 1],
                                  ALU.is_equal, ALU.mult)
                then(last)
                for b in range(2):
                    for e in range(NE):
                        c = b * NE + e
                        last = TS(gated[:, b, e, :], onehot[:, b, e, :], gates[:, c:c + 1], None, ALU.mult)
                last.then_inc(oh_ready, 1)
                dve.wait_ge(cb_kept, 4 * p + 4)
                dve.wait_ge(act_turned, 8)

                def split(kind, j, at1):
                    for q in range(4):
                        c = 4 * place_of[(kind, j)] + q
                        dve.wait_ge(hi_ready, at1 * PIECES_E + (c + 1))
                        raw = ring[:, e_slot[c // 2], c % 2 * PIECE:(c % 2 + 1) * PIECE]
                        TT(w_lo[:, q, :], raw, w_hi[:, q, :].bitcast(F32), ALU.subtract).then_inc(lo_ready, 1)

                def gathered(at1):
                    for f in range(2):
                        dve.wait_ge(ga_kept, at1 * 2 + (f + 1))
                        fs = slice(f * CW, (f + 1) * CW)
                        TT(xg_lo[:, fs], bank[1 + 2 * f][:, :], xg_hi[:, fs].bitcast(F32), ALU.subtract).then_inc(
                            ga_low, 1)

                def multiply(j, at1):
                    dve.wait_ge(sl_done, at1 * NJ + (j + 1))
                    dve.wait_ge(pc_free, at1 * PIECES_E + (4 * (place_of[("u", j)] + 1) + PIECES))
                    if j >= 2:
                        dve.wait_ge(at_done, at1 * NJ + (j - 1))
                    TT(act_b[j % 2], sil_b[j % 2], bank[2 + j % 2][:, :], ALU.mult).then_inc(ac_ready, 1)

                def turned(j, at1):
                    dve.wait_ge(at_kept, at1 * NJ + (j + 1))
                    TT(at_lo[:, j % 2, :], bank[6][:, :], at_hi[:, j % 2, :].bitcast(F32), ALU.subtract).then_inc(
                        at_low, 1)

                def add(at1):
                    for f in range(4):
                        b, hf = f // 2, f % 2
                        dve.wait_ge(sct_done, at1 * 4 + (f + 1))
                        o = x_tok[:, b, hf * 512:(hf + 1) * 512]
                        TT(o, o, bank[(6, 7, 4, 5)[f]][:, :], ALU.add).then_inc(sct_added, 1)

                def expert(e, at1, last_one):
                    dve.tensor_copy(combine_e, combine[:, e, :]).then_inc(cbe_ready, 1)
                    split("g", 1, at1)
                    multiply(0, at1)
                    split("u", 1, at1)
                    turned(0, at1)
                    split("d", 0, at1)
                    for j in range(2, NJ):
                        multiply(j - 1, at1)
                        split("g", j, at1)
                        split("u", j, at1)
                        turned(j - 1, at1)
                        split("d", j - 1, at1)
                    multiply(NJ - 1, at1)
                    split("d", NJ - 1, at1)
                    turned(NJ - 1, at1)
                    if not last_one:
                        gathered(at1 + 1)
                        split("g", 0, at1 + 1)
                        split("u", 0, at1 + 1)
                    add(at1)
                    dve.wait_ge(sct_added, at1 * 4 + 4)

                first = p * NE
                gathered(first)
                split("g", 0, first)
                split("u", 0, first)
                with dve.Fori(0, NE - 1) as e:
                    expert(e, e + first, False)
                expert(NE - 1, first + NE - 1, True)

            moe_pass(0)
            over_full = dve.value_load(flag[0:1, 0:1])
            with dve.If(over_full > 0):
                moe_pass(1)
            dve.memset(small[:, 0:1], 0.0).then_inc(moe_done, 1)


_OUT = "out"


def kernel(**inputs):
    import concourse.bacc as bacc
    from concourse.bass_utils import run_bass_kernel_spmd

    a = {k: np.asarray(v) for k, v in inputs.items()}

    def columns(v):
        return np.stack([r.reshape(-1, P).T for r in v.reshape(L, -1)])

    def twice(v):
        return np.concatenate([v, v], axis=1).reshape(L, P, 1)

    vres_rows = np.zeros((L, P, 4), np.float32)
    vres_rows[1, 0:16, 0] = a["vres_mu"][0]
    vres_rows[1, :, 1:4] = a["vres_v0"][0].reshape(NRT, P).T
    params = np.concatenate([
        columns(a["mix_norm"]), columns(a["tshift_mu"]), columns(a["decay_w0"]), columns(a["iclr_a0"]),
        columns(a["k_k"]), columns(a["k_a"]), columns(a["r_k"]), columns(a["ln_x_w"]), columns(a["ln_x_b"]),
        columns(a["conv_w"]), columns(a["conv_out_norm"]), twice(a["q_norm"]), twice(a["k_norm"]),
        columns(a["attn_out_norm"]), columns(a["ffn_norm"]), vres_rows], axis=2)
    assert params.shape[2] == N_PARAM
    consts, masks = constant_tables()
    arrays = {
        "x": a["x"][0], "consts": consts, "masks": masks,
        "params": np.ascontiguousarray(params.transpose(1, 0, 2)).reshape(P, L * N_PARAM),
        "lora": np.concatenate([a["decay_w2"], a["iclr_a2"], a["gate_g2"]], axis=1),
        "vres_v2": a["vres_v2"][0], "w_in": a["w_in"], "vres_w": a["vres_w_in"][0], "w_o": a["w_o"],
        "dense_wg": a["dense_wg"], "dense_wu": a["dense_wu"], "dense_wd": a["dense_wd"],
        "router": a["router"][0], "moe_wg": a["moe_wg"][0], "moe_wu": a["moe_wu"][0], "moe_wd": a["moe_wd"][0],
    }
    nc = bacc.Bacc("TRN2", target_bir_lowering=False, num_devices=1)
    feed, aps = {}, []
    for name, v in arrays.items():
        v = np.ascontiguousarray(v)
        feed["in_" + name] = v
        aps.append(nc.dram_tensor("in_" + name, v.shape, mybir.dt.from_np(v.dtype), kind="ExternalInput").ap())
    result = nc.dram_tensor(_OUT, (T, D), F32, kind="ExternalOutput").ap()
    decoder_trunk(nc, *aps, result)
    r = run_bass_kernel_spmd(nc, [feed], core_ids=[0])
    return r.results[0][_OUT].reshape(1, T, D)
```

```python
from contextlib import ExitStack

import numpy as np

import concourse.bass as bass
from concourse import mybir

F32 = mybir.dt.float32
F32R = mybir.dt.float32r
I32 = mybir.dt.int32
U8 = mybir.dt.uint8
ALU = mybir.AluOpType
ACT = mybir.ActivationFunctionType
AX = mybir.AxisListType

P = 128
D = 1024
T = 256
L = 2
KT = D // P
RW = 384
NRT = RW // P
HEADS = 6
HD = 64
N_IN = 3200
F = 3584
NE = 8
C = 64
NC = T // C
CW = 512
NJ = F // CW
HALF = KT * CW // 2
SLOTS = 6
FIRST_OVER = 3
PIECE = HALF // 2
PIECES = 4
NORM_EPS = 1e-6
GN_EPS = 64e-5
DECAY = float(np.exp(-0.5))
SEL_ROWS = 12

CONST_COLS = {}
_at = 0
for _name, _n in (("ident", P), ("ones", P), ("pair", P), ("rot", P), ("cos", T), ("sin", T), ("strict", P),
                  ("incl", P), ("bias", 3 * P), ("iota", P), ("tri", P), ("selin", 6 * SEL_ROWS), ("selout", 6 * P)):
    CONST_COLS[_name] = (_at, _n)
    _at += _n
N_CONST = _at

PARAM_COLS = {}
_at = 0
for _name, _n in (("mix_norm", 8), ("mu", 10), ("w0", 3), ("a0", 3), ("k_k", 3), ("k_a", 3), ("r_k", 3), ("ln_w", 3),
                  ("ln_b", 3), ("conv_w", 6), ("conv_g", 2), ("q_g", 1), ("k_g", 1), ("out_g", 3), ("ffn_norm", 8),
                  ("vres_mu", 1), ("vres_v0", 3)):
    PARAM_COLS[_name] = (_at, _n)
    _at += _n
N_PARAM = _at


def constant_tables():
    c = np.zeros((P, N_CONST), np.float32)

    def put(name, a):
        at, n = CONST_COLS[name]
        c[:a.shape[0], at:at + n] = a

    i = np.arange(P)
    put("ident", np.eye(P))
    put("ones", np.ones((P, P)))
    put("pair", i[:, None] // HD == i[None, :] // HD)
    rot = np.zeros((P, P))
    for m in range(P):
        if m % HD < HD // 2:
            rot[m + HD // 2, m] = -1.0
        else:
            rot[m - HD // 2, m] = 1.0
    put("rot", rot)
    inv_freq = np.float32(10000.0) ** (-np.arange(HD // 2, dtype=np.float32) * np.float32(2.0) / np.float32(HD))
    ang = np.arange(T, dtype=np.float32)[None, :] * inv_freq.astype(np.float32)[i % (HD // 2)][:, None]
    put("cos", np.cos(ang))
    put("sin", np.sin(ang))
    same = i[:, None] // C == i[None, :] // C
    put("strict", same & (i[:, None] < i[None, :]))
    put("incl", same & (i[:, None] <= i[None, :]))
    q, k = np.arange(T)[:, None], np.arange(T)[None, :]
    seen = np.zeros((T, T))
    for window, dil in ((128, 1), (512, 4), (2048, 16)):
        seen += (q >= k) & (q - k <= window) & ((q - k) % dil == 0)
    bias = np.where(seen > 0, np.log(np.maximum(seen, 1)), -1e30)
    put("bias", np.concatenate([bias[:P, :P], bias[P:, :]], axis=1))
    put("iota", np.tile(i, (P, 1)))
    put("tri", i[:, None] < i[None, :])
    selin = np.zeros((P, 6, SEL_ROWS))
    selout = np.zeros((SEL_ROWS, 6, P))
    for t in range(6):
        for m in range(P):
            selin[m, t, 2 * t + m // HD] = 1.0
            selout[2 * t + m // HD, t, m] = 1.0
    put("selin", selin.reshape(P, -1))
    put("selout", selout.reshape(SEL_ROWS, -1))
    masks = np.zeros((P, 2, 6, P), np.float32)
    for lev in range(6):
        b = 1 << lev
        m = (i[:, None] // (2 * b) == i[None, :] // (2 * b)) & (i[:, None] // b % 2 == 1) & (i[None, :] // b % 2 == 0)
        masks[:, 0, lev] = m
        masks[:, 1, lev] = m.T
    return c, masks.reshape(P, -1)


def decoder_trunk(nc, x, consts, masks, params, lora, vres_v2, w_in, vres_w, w_o, dense_wg, dense_wu, dense_wd,
                  router, moe_wg, moe_wu, moe_wd, out):
    with ExitStack() as ctx:
        def sem(name):
            return ctx.enter_context(nc.semaphore(name))

        ring = ctx.enter_context(nc.sbuf_tensor("ring", [P, SLOTS, HALF], F32))
        ARENA = 26100
        arena = ctx.enter_context(nc.sbuf_tensor("arena", [P, ARENA], F32))
        mask8 = ctx.enter_context(nc.sbuf_tensor("mask8", [P, 12 * P], U8))
        flag = ctx.enter_context(nc.sbuf_tensor("flag", [P, 1], I32))
        w_hi = ctx.enter_context(nc.sbuf_tensor("w_hi", [P, PIECES, PIECE], F32R))
        w_lo = ctx.enter_context(nc.sbuf_tensor("w_lo", [P, PIECES, PIECE], F32R))
        acts_hi = ctx.enter_context(nc.sbuf_tensor("acts_hi", [P, KT * T], F32R))
        acts_lo = ctx.enter_context(nc.sbuf_tensor("acts_lo", [P, KT * T], F32R))
        da_hi = ctx.enter_context(nc.sbuf_tensor("da_hi", [P, 4 * T], F32R))
        da_lo = ctx.enter_context(nc.sbuf_tensor("da_lo", [P, 4 * T], F32R))
        bank = [ctx.enter_context(nc.psum_tensor(f"bank{b}", [P, 512], F32)) for b in range(8)]

        h_hi, h_lo = (a[:, :].rearrange("p (k t) -> p k t", k=KT) for a in (acts_hi, acts_lo))
        xg_hi, xg_lo = (a[:, 0:KT * P] for a in (acts_hi, acts_lo))
        at_hi, at_lo = (a[:, KT * P:KT * T].rearrange("p (b n) -> p b n", b=2) for a in (acts_hi, acts_lo))

        class Region:

            def __init__(self, ap, size):
                self.ap, self.size, self.at = ap, size, 0

            def take(self, n):
                a = self.at
                self.at += n
                assert self.at <= self.size, (self.at, self.size)
                return self.ap[:, a:a + n]

        keep = Region(arena[:, :], ARENA)
        cst = keep.take(N_CONST)
        prm = keep.take(L * N_PARAM)
        lora_w = keep.take(L * RW).rearrange("p (l n) -> p l n", l=L)
        v2w = keep.take(RW)
        vres_wt = keep.take(KT * 16).rearrange("p (k n) -> p k n", k=KT)
        router_w = keep.take(KT * NE).rearrange("p (k n) -> p k n", k=KT)
        xT = keep.take(KT * T).rearrange("p (k t) -> p k t", k=KT)
        hT = keep.take(KT * T).rearrange("p (k t) -> p k t", k=KT)
        rn = keep.take(T)
        small = keep.take(320)
        top_gap = small[:, 160:162]
        phase = keep.at

        pT = keep.take(22 * T).rearrange("p (k t) -> p k t", k=22)
        v_att = keep.take(2 * RW).rearrange("p (b n) -> p b n", b=2)
        v_first = keep.take(NRT * T).rearrange("p (i t) -> p i t", i=NRT)
        w65 = keep.take(NRT * NC * (C + 1)).rearrange("p (i c t) -> p i c t", i=NRT, c=NC)
        gram = [keep.take(HEADS * P).rearrange("p (h t) -> p h t", h=HEADS) for _ in range(4)]
        inv_w, a_gate, tmp1, tmp2 = [g.rearrange("p h t -> p (h t)").rearrange("p (i t) -> p i t", i=NRT)
                                     for g in gram]
        g_gate = keep.take(NRT * T).rearrange("p (i t) -> p i t", i=NRT)
        bonus = keep.take(NRT * T).rearrange("p (i t) -> p i t", i=NRT)
        tok_all = keep.take(4 * RW)
        tok = [tok_all[:, n * RW:(n + 1) * RW] for n in range(4)]
        lora_in = keep.take(T)
        pv = keep.take(T)
        state = arena[:, keep.at - 2 * T:keep.at - 2 * T + RW].rearrange("p (i v) -> p i v", i=NRT)
        head_rn = keep.take(T)
        sq_qk = keep.take(6 * T).rearrange("p (k t) -> p k t", k=6)
        o_tok = sq_qk.rearrange("p k t -> p (k t)")[:, 0:2 * RW].rearrange("p (b h d) -> p b h d", b=2, h=HEADS)
        o_sq = sq_qk.rearrange("p k t -> p (k t)")[:, 2 * RW:4 * RW].rearrange("p (b h d) -> p b h d", b=2, h=HEADS)
        probs = [keep.take(3 * P) for _ in range(2)]
        assert keep.at <= ARENA
        kk = tok_all[:, 0:2 * RW].rearrange("p (i t) -> p i t", i=NRT)
        sig_w = tok_all[:, 2 * RW:4 * RW].rearrange("p (i t) -> p i t", i=NRT)
        aT = hT[:, 0:3, :]
        bT = hT[:, 3:6, :]

        over = Region(ring[:, FIRST_OVER:SLOTS, :].rearrange("p s n -> p (s n)"), (SLOTS - FIRST_OVER) * HALF)
        inv = over.take(HEADS * P).rearrange("p (h t) -> p h t", h=HEADS)
        invT = over.take(HEADS * P).rearrange("p (h t) -> p h t", h=HEADS)
        lt = over.take(HEADS * P).rearrange("p (h t) -> p h t", h=HEADS)
        lv = over.take(RW)
        p1 = over.take(RW)
        u_tok = over.take(RW)
        y_cross = over.take(RW)
        y_tok = over.take(RW)
        state_tmp = over.take(RW).rearrange("p (i v) -> p i v", i=NRT)
        end_w = over.take(RW).rearrange("p (i v) -> p i v", i=NRT)
        ta_t = over.take(RW).rearrange("p (i t) -> p i t", i=NRT)
        probs_t = over.take(3 * P)
        conv_tmp = over.take(T)
        moe = Region(arena[:, phase:ARENA], ARENA - phase)
        x_tok = moe.take(2 * D).rearrange("p (b d) -> p b d", b=2)
        h_tok = moe.take(2 * D).rearrange("p (b d) -> p b d", b=2)
        onehot = moe.take(2 * NE * P).rearrange("p (b e s) -> p b e s", b=2, e=NE)
        gated = moe.take(2 * NE * P).rearrange("p (b e s) -> p b e s", b=2, e=NE)
        combine = moe.take(NE * T).rearrange("p (e t) -> p e t", e=NE)
        combine_e = moe.take(T)
        act_b = [moe.take(CW) for _ in range(2)]
        sil_b = [moe.take(CW) for _ in range(2)]
        dense = Region(arena[:, phase:ARENA], ARENA - phase)
        dense_sil = dense.take(4 * T)
        dense_act = dense.take(4 * T)
        assert dense.at <= 22 * T + 2 * RW
        mask_in = sq_qk.rearrange("p k t -> p (k t)")
        gated_all = gated.rearrange("p b e s -> p (b e s)")
        yg = gated_all[:, D:2 * D]

        def da_parts(j):
            if j == NJ - 1:
                return acts_hi[:, 0:4 * T], acts_lo[:, 0:4 * T]
            return da_hi[:, :], da_lo[:, :]

        def const(name, rows=P):
            at, n = CONST_COLS[name]
            return cst[0:rows, at:at + n]

        def param(l, name, i=0):
            at = l * N_PARAM + PARAM_COLS[name][0] + i
            return prm[:, at:at + 1]

        def spread(ap, n):
            return ap.rearrange("p (a m) -> p a m", a=1).to_broadcast([ap.shape[0], n, ap.shape[1]])

        def stretch(ap, n):
            return ap.rearrange("p (m a) -> p m a", a=1).to_broadcast([ap.shape[0], ap.shape[1], n])

        def lane(h):
            return h % 2 * 3 + h // 2

        ident = const("ident")
        ones = const("ones")
        selin = const("selin").rearrange("p (t m) -> p t m", t=6)
        selout = const("selout", SEL_ROWS).rearrange("p (t m) -> p t m", t=6)
        lmask = mask8[:, :].rearrange("p (a l m) -> p a l m", a=2, l=6)

        x_in = sem("x_in")
        ident_in = sem("ident_in")
        consts_in = sem("consts_in")
        inputs_in = sem("inputs_in")
        ring_in = [sem(f"ring_in{s}") for s in range(SLOTS)]
        hi_ready = sem("hi_ready")
        lo_ready = sem("lo_ready")
        pc_free = sem("pc_free")
        x_turned = sem("x_turned")
        x_kept = sem("x_kept")
        sq_ready = sem("sq_ready")
        ss_ready = sem("ss_ready")
        ms_ready = sem("ms_ready")
        rn_ready = sem("rn_ready")
        h_ready = sem("h_ready")
        unit_done = sem("unit_done")
        unit_kept = sem("unit_kept")
        lora_ready = sem("lora_ready")
        vres_shifted = sem("vres_shifted")
        lora_act = sem("lora_act")
        lora_done = sem("lora_done")
        lora_kept = sem("lora_kept")
        cs_ready = sem("cs_ready")
        w_ready = sem("w_ready")
        hs_sq = sem("hs_sq")
        hs_sum = sem("hs_sum")
        hs_rec = sem("hs_rec")
        hs_root = sem("hs_root")
        hs_bc = sem("hs_bc")
        hs_used = sem("hs_used")
        qk_sq = sem("qk_sq")
        bonus_in = sem("bonus_in")
        bonus_sum = sem("bonus_sum")
        bonus_ready = sem("bonus_ready")
        rw_ready = sem("rw_ready")
        rot_done = sem("rot_done")
        rope_ready = sem("rope_ready")
        state_zero = sem("state_zero")
        inv_init = sem("inv_init")
        tok_done = sem("tok_done")
        tok_kept_a = sem("tok_kept_a")
        tok_kept_d = sem("tok_kept_d")
        gram_done = sem("gram_done")
        gram_kept = sem("gram_kept")
        lv_done = sem("lv_done")
        lv_kept = sem("lv_kept")
        lt_done = sem("lt_done")
        lt_kept = sem("lt_kept")
        tlt_done = sem("tlt_done")
        inv_ready = sem("inv_ready")
        p1_done = sem("p1_done")
        p1_kept = sem("p1_kept")
        ta_kept = sem("ta_kept")
        u_done = sem("u_done")
        u_ready = sem("u_ready")
        yc_done = sem("yc_done")
        yc_kept = sem("yc_kept")
        st_done = sem("st_done")
        st_ready = sem("st_ready")
        y_done = sem("y_done")
        gn_rec = sem("gn_rec")
        gn_root = sem("gn_root")
        yn_ready = sem("yn_ready")
        yt_done = sem("yt_done")
        y_out = sem("y_out")
        sc_done = sem("sc_done")
        sc_read = sem("sc_read")
        mx_ready = sem("mx_ready")
        ex_done = sem("ex_done")
        tp_done = sem("tp_done")
        tp_kept = sem("tp_kept")
        pv_done = sem("pv_done")
        o_ready = sem("o_ready")
        on_rec = sem("on_rec")
        on_root = sem("on_root")
        on_ready = sem("on_ready")
        ot_done = sem("ot_done")
        att_out = sem("att_out")
        wo_done = sem("wo_done")
        wo_added = sem("wo_added")
        h_high = sem("h_high")
        h_low = sem("h_low")
        ds_done = sem("ds_done")
        da_ready = sem("da_ready")
        da_high = sem("da_high")
        da_low = sem("da_low")
        x_ffn = sem("x_ffn")
        logit_done = sem("logit_done")
        pe_turned = sem("pe_turned")
        act_turned = sem("act_turned")
        route_sel = sem("route_sel")
        rank_done = sem("rank_done")
        route_act = sem("route_act")
        route_exp = sem("route_exp")
        flag_ready = sem("flag_ready")
        oh_ready = sem("oh_ready")
        gated_ready = sem("gated_ready")
        cb_done = sem("cb_done")
        cb_kept = sem("cb_kept")
        ga_done = sem("ga_done")
        ga_kept = sem("ga_kept")
        ga_low = sem("ga_low")
        gt_done = sem("gt_done")
        up_done = sem("up_done")
        sl_done = sem("sl_done")
        ac_ready = sem("ac_ready")
        at_done = sem("at_done")
        at_kept = sem("at_kept")
        at_low = sem("at_low")
        dn_done = sem("dn_done")
        yg_kept = sem("yg_kept")
        cbe_ready = sem("cbe_ready")
        sct_done = sem("sct_done")
        sct_added = sem("sct_added")
        moe_done = sem("moe_done")
        out_done = sem("out_done")
        dve_step = sem("dve_step")
        act_step = sem("act_step")
        pool_step = sem("pool_step")

        CHUNKS = (4, 5, 6, 2, 0, 1, 3)
        N_UNITS = (26, 27)
        UNIT0 = (0, 26)
        LORAS = (3, 4)
        LORA0 = (0, 3)

        def units(l):
            got = []
            for place, ch in enumerate(CHUNKS):
                mine = [("cm", n) for n in range(4 * ch, 4 * ch + 4) if n < 22]
                if ch == 5:
                    mine += [("va", 0), ("va", 1)]
                if ch == 6:
                    mine = [("vb", 0), ("vb", 1)] + ([("vres", 0)] if l else [])
                got += [(place, *m, i == 0, i == len(mine) - 1) for i, m in enumerate(mine)]
            return got

        SPLIT_IN = (2, 1)
        IN0 = {(l, ch): l * 4 * (len(SPLIT_IN) + 3 * NJ) + 4 * i
               for l in range(L) for i, ch in enumerate(SPLIT_IN)}
        DENSE0 = 4 * len(SPLIT_IN)
        MOE0 = 2 * DENSE0 + 4 * 3 * NJ

        def kept(l, kind, n):
            return UNIT0[l] + [u[1:3] for u in units(l)].index((kind, n)) + 1

        ORDER = [("g", 0), ("u", 0)]
        for _j in range(1, NJ):
            ORDER += [("g", _j), ("u", _j), ("d", _j - 1)]
        ORDER += [("d", NJ - 1)]

        stream = []
        for l in range(L):
            us = units(l)
            for place, ch in enumerate(CHUNKS):
                seen = UNIT0[l] + max(i for i, u in enumerate(us) if u[0] == place) + 1
                stream += [("in", l, ch, hf, (unit_done, seen)) for hf in range(2)]
            for ch in range(2):
                stream += [("o", l, ch, hf, (wo_done, 8 * l + 4 * (ch + 1))) for hf in range(2)]
            if l == 0:
                for place, (kind, j) in enumerate(ORDER):
                    stream += [(kind, l, j, hf, (lo_ready, DENSE0 + 4 * place + 2 * hf + 2)) for hf in range(2)]
        slot_of, count_of, before = [], [], []
        filled, user, at_slot = [0] * SLOTS, [None] * SLOTS, 0
        for n, item in enumerate(stream):
            if item[0] == "o" and stream[n - 1][0] == "in":
                at_slot = 0
            filled[at_slot] += 1
            slot_of.append(at_slot)
            count_of.append(16 * filled[at_slot])
            before.append(user[at_slot])
            user[at_slot] = n
            at_slot = (at_slot + 1) % SLOTS
        halves = {item[:4]: n for n, item in enumerate(stream)}

        EXPERT = [(kind, j, hf) for kind, j in ORDER for hf in range(2)]
        PER_E = len(EXPERT)
        FILLS = PER_E // SLOTS
        assert PER_E % SLOTS == 0
        e_slot = [(at_slot + i) % SLOTS for i in range(PER_E)]
        PIECES_E = 2 * PER_E
        e_count = [16 * (filled[e_slot[i]] + i // SLOTS + 1) for i in range(PER_E)]
        e_before = [user[e_slot[i]] for i in range(SLOTS)]
        place_of = {key: i for i, key in enumerate(ORDER)}

        def half_cols(slot):
            return ring[:, slot, :].rearrange("p (k c) -> p k c", k=KT // 2)

        def half_rows(slot):
            return ring[:, slot, :].rearrange("p (i c) -> p i c", i=2)

        TOK_BANKS = (0, 1, 6, 7)
        SUM_BANKS = (7, 7, 3, 7)
        TURN_AT = 2
        N_INPUTS = 5
        RWKV, OTHERS = range(0, NRT), range(NRT, KT)
        y_tiles = [0, 1, 2, 10, 11, 16, 17, 18]

        block = ctx.enter_context(nc.Block())

        @block.sync
        def _(sp):
            sp.dma_start(x_tok, x.rearrange("(b p) d -> p b d", p=P)).then_inc(x_in, 16)
            sp.dma_start(cst[:, 0:2 * P], consts[:, 0:2 * P]).then_inc(ident_in, 16)
            sp.dma_start(cst[:, 2 * P:N_CONST], consts[:, 2 * P:N_CONST]).then_inc(consts_in, 16)
            sp.dma_start(prm, params).then_inc(consts_in, 16)

            def fetch(kind, slot, w, j, hf):
                if kind == "d":
                    r0 = CW * j + hf * 2 * P
                    return sp.dma_start(half_rows(slot), w[r0:r0 + 2 * P, :].rearrange("(i p) n -> p i n", p=P))
                lo, hi = CW * j, min(CW * (j + 1), w.shape[1])
                rows = w[hf * 4 * P:(hf + 1) * 4 * P, lo:hi]
                return sp.dma_start(half_cols(slot)[:, :, 0:hi - lo], rows.rearrange("(k p) n -> p k n", p=P))

            def mixers_done(l):
                sp.wait_ge(y_out, 2 * l + 2)
                sp.wait_ge(att_out, l + 1)

            for n, (kind, l, j, hf, _) in enumerate(stream):
                slot = slot_of[n]
                if before[n] is not None:
                    sp.wait_ge(*stream[before[n]][4])
                    if stream[before[n]][0] == "in" and kind != "in" and slot >= FIRST_OVER:
                        mixers_done(l)
                w = {"in": w_in[l], "o": w_o[l], "g": dense_wg[0], "u": dense_wu[0], "d": dense_wd[0]}[kind]
                fetch(kind, slot, w, j, hf).then_inc(ring_in[slot], 16)

            def load_expert(e, i):
                kind, j, hf = EXPERT[i]
                w = {"g": moe_wg, "u": moe_wu, "d": moe_wd}[kind]
                fetch(kind, e_slot[i], w[e], j, hf).then_inc(ring_in[e_slot[i]], 16)

            AHEAD = EXPERT.index(("d", 0, 0)) + 1

            def moe_pass(p):
                base = MOE0 // 2 + p * NE * PER_E
                for i in range(SLOTS):
                    if p:
                        sp.wait_ge(lo_ready, 2 * (base + i - SLOTS + 1))
                    else:
                        sp.wait_ge(*stream[e_before[i]][4])
                        if e_slot[i] >= FIRST_OVER:
                            mixers_done(L - 1)
                    load_expert(0, i)
                for i in range(SLOTS, AHEAD):
                    sp.wait_ge(lo_ready, 2 * (base + i - SLOTS + 1))
                    load_expert(0, i)
                with sp.Fori(0, NE - 1) as e:
                    done = e * PIECES_E + 2 * base
                    for i in range(AHEAD, PER_E + AHEAD):
                        sp.wait_ge(lo_ready, done + 2 * (i - SLOTS + 1))
                        load_expert(e + i // PER_E, i % PER_E)
                for i in range(AHEAD, PER_E):
                    sp.wait_ge(lo_ready, 2 * (base + (NE - 1) * PER_E + i - SLOTS + 1))
                    load_expert(NE - 1, i)

            moe_pass(0)
            sp.wait_ge(flag_ready, 1)
            over_full = sp.value_load(flag[0:1, 0:1])
            with sp.If(over_full > 0):
                moe_pass(1)

        @block.gpsimd
        def _(pool):
            pool_steps = [0]

            def then(ins):
                pool_steps[0] += 1
                ins.then_inc(pool_step, 1)
                pool.wait_ge(pool_step, pool_steps[0])

            def convolution(l):
                pool.wait_ge(unit_kept, UNIT0[l] + N_UNITS[l])
                cu, cy, cb = pT[:, 14:16, :], pT[:, 12:14, :], pT[:, 10:12, :]
                then(pool.tensor_tensor(cu, cy, cu, ALU.mult))
                for i in range(2):
                    last = pool.tensor_scalar(cy[:, i, :], cu[:, i, :], param(l, "conv_w", 4 + i), None, ALU.mult)
                then(last)
                for back in (1, 2):
                    for i in range(2):
                        then(pool.tensor_scalar(conv_tmp[:, back:T], cu[:, i, 0:T - back],
                                                param(l, "conv_w", 2 * (2 - back) + i), None, ALU.mult))
                        then(pool.tensor_tensor(cy[:, i, back:T], cy[:, i, back:T], conv_tmp[:, back:T], ALU.add))
                then(pool.tensor_tensor(cy, cy, cb, ALU.mult))
                pool.tensor_tensor(cu, cy, cy, ALU.mult).then_inc(hs_sq, 1)

            pool.wait_ge(ident_in, 16)
            pool.wait_ge(consts_in, 32)
            for l in range(L):
                pool.wait_ge(unit_done, UNIT0[l] + N_UNITS[l])
                if l:
                    pool.wait_ge(x_ffn, 4)
                pool.memset(state, 0.0).then_inc(state_zero, 1)
                for tau in range(2):
                    q = 2 * l + tau
                    if q:
                        pool.wait_ge(p1_done, q)
                    if l and not tau:
                        pool.wait_ge(unit_done, UNIT0[l] + N_UNITS[l])
                    pool.tensor_copy(inv, spread(ident, HEADS)).then_inc(inv_init, 1)
                    pool.tensor_copy(invT, spread(ident, HEADS)).then_inc(inv_init, 1)
                    if not tau:
                        convolution(l)

        @block.tensor
        def _(pe):
            def mm(out_, lhsT, rhs, start=True, stop=True):
                return pe.matmul(out_, lhsT, rhs, start=start, stop=stop)

            pe.wait_ge(x_in, 16)
            pe.wait_ge(ident_in, 16)
            for i in range(4):
                for k in range(2):
                    for b in range(2):
                        c0 = k * T + b * P
                        last = pe.transpose(bank[i][:, c0:c0 + P], x_tok[:, b, (2 * i + k) * P:(2 * i + k + 1) * P],
                                            ident)
                        if i == k == b == 0:
                            last.then_inc(pc_free, PIECES)
                last.then_inc(x_turned, 1)

            def three(out_, a_hi, a_lo, b_hi, b_lo, first, final, **kw):
                pe.matmul(out_, a_hi, b_hi, start=first, stop=False, **kw)
                pe.matmul(out_, a_hi, b_lo, start=False, stop=False, **kw)
                return pe.matmul(out_, a_lo, b_hi, start=False, stop=final, **kw)

            def sum_squares(n, k):
                pe.wait_ge(sq_ready, KT * n + k + 1)
                last = mm(bank[SUM_BANKS[n]][:, 0:T], ones, hT[:, k, :], k == 0, k == KT - 1)
                if k == KT - 1:
                    last.then_inc(ss_ready, 1)

            def norm(n):
                for k in range(KT):
                    sum_squares(n, k)

            conv_sq = [pT[:, 14, :], pT[:, 15, :]]

            def head_sum(n, tiles, b):
                for t, sq in enumerate(tiles):
                    last = mm(bank[b][0:SEL_ROWS, 0:T], selin[:, t, :], sq, t == 0, t == len(tiles) - 1)
                last.then_inc(hs_sum, 1)

            def head_spread(n, n_tiles, banks):
                pe.wait_ge(hs_root, n + 1)
                for t in range(n_tiles):
                    last = mm(bank[banks[t // 2]][:, t % 2 * T:t % 2 * T + T], selout[:, t, :],
                              head_rn[0:SEL_ROWS, :])
                last.then_inc(hs_bc, 1)

            def project(l, place, kind, n, first, final, u):
                g = UNIT0[l] + u
                ch = CHUNKS[place]
                ns = [halves[("in", l, ch, hf)] for hf in range(2)]
                if first and ch in SPLIT_IN:
                    pe.wait_ge(lo_ready, IN0[l, ch] + 4)
                    pe.wait_ge(h_low, KT * (2 * l + 1))
                elif first:
                    for m in ns:
                        pe.wait_ge(ring_in[slot_of[m]], count_of[m])
                if g >= 4:
                    pe.wait_ge(unit_kept, g - 3)
                b = bank[g % 4]
                for k in range(KT):
                    w = half_cols(slot_of[ns[k // 4]])[:, k % 4, :]
                    if u == 0:
                        pe.wait_ge(h_ready, KT * 2 * l + k + 1)
                    if ch in SPLIT_IN:
                        ws = slice(k % 2 * CW + n % 4 * P, k % 2 * CW + (n % 4 + 1) * P)
                        last = three(b[:, 0:T], w_hi[:, k // 2, ws], w_lo[:, k // 2, ws], h_hi[:, k, :], h_lo[:, k, :],
                                     k == 0, k == KT - 1)
                    elif kind == "cm":
                        c0 = n % 4 * P
                        last = mm(b[:, 0:T], w[:, c0:c0 + P], hT[:, k, :], k == 0, k == KT - 1)
                    elif kind == "vres":
                        last = mm(b[0:16, 0:T], vres_wt[:, k, :], hT[:, k, :], k == 0, k == KT - 1)
                    else:
                        h = hT[:, k, n * P:(n + 1) * P]
                        if kind == "va":
                            last = mm(b[:, 0:T], h, w[:, 2 * P:4 * P], k == 0, k == KT - 1)
                        else:
                            last = mm(b[:, 0:P], h, w[:, 0:P], k == 0, k == KT - 1)
                last.then_inc(unit_done, 1)

            def lora_product(kind, l, banks):
                for i in range(NRT):
                    o = bank[banks[i // 2]][:, i % 2 * T:i % 2 * T + T]
                    cols = slice(i * P, (i + 1) * P)
                    if kind == "v":
                        last = mm(o, v2w[0:16, cols], pv[0:16, :])
                    else:
                        r0, r1 = {"w": (0, 32), "a": (32, 64), "g": (64, 128)}[kind]
                        last = mm(o, lora_w[r0:r1, l, cols], lora_in[r0:r1, :])
                last.then_inc(lora_done, 1)

            def out_weights(l, ch):
                for hf in range(2):
                    n = halves[("o", l, ch, hf)]
                    pe.wait_ge(ring_in[slot_of[n]], count_of[n])

            def out_product(l, m, tiles, first, final):
                for k in tiles:
                    w = half_cols(slot_of[halves[("o", l, m // 4, k // 4)]])[:, k % 4, m % 4 * P:(m % 4 + 1) * P]
                    last = mm(bank[m % 4][:, 0:T], w, pT[:, y_tiles[k], :], first and k == tiles[0],
                              final and k == tiles[-1])
                return last

            def token_major(tau):
                ts = slice(tau * P, (tau + 1) * P)
                for b0, src in zip(TOK_BANKS, (aT, bT, pT[:, 3:6, :], pT[:, 6:9, :])):
                    for i in range(NRT):
                        last = pe.transpose(bank[b0][:, i * P:(i + 1) * P], src[:, i, ts], ident)
                    last.then_inc(tok_done, 1)

            def recurrence(l, tau):
                q = 2 * l + tau
                ts = slice(tau * P, (tau + 1) * P)
                kT, vT, rT = pT[:, 3:6, :], pT[:, 6:9, :], pT[:, 0:3, :]
                if tau:
                    pe.wait_ge(y_out, q)
                else:
                    pe.wait_ge(rw_ready, l + 1)
                    pe.wait_ge(unit_kept, UNIT0[l] + N_UNITS[l])
                    token_major(tau)
                pe.wait_ge(bonus_ready, l + 1)
                for n, (x1, x2, b0) in enumerate(((bT, aT, 4), (aT, bT, 6), (kT, aT, 4), (bT, rT, 6), (kT, rT, 4))):
                    if n == 1:
                        pe.wait_ge(tok_kept_d, 2 * q + 2)
                    if n == 2:
                        pe.wait_ge(gram_kept, 4 * q + 1)
                    if n == 3:
                        pe.wait_ge(inv_ready, 12 * q + 2)
                    if n == 4:
                        pe.wait_ge(gram_kept, 4 * q + 2)
                    for h in range(HEADS):
                        r = slice(h % 2 * HD, h % 2 * HD + HD)
                        last = mm(bank[b0 + h % 2][:, h // 2 * P:(h // 2 + 1) * P], x1[r, h // 2, ts], x2[r, h // 2, ts])
                    last.then_inc(gram_done, 1)
                pe.wait_ge(gram_kept, 4 * q + 3)
                pe.wait_ge(tok_kept_d, 2 * q + 2)
                for h in range(HEADS):
                    last = mm(bank[6][:, h * HD:(h + 1) * HD], gram[1][:, lane(h), :], tok[3][:, h * HD:(h + 1) * HD])
                last.then_inc(lv_done, 1)
                pe.wait_ge(gram_kept, 4 * q + 4)
                pe.wait_ge(tok_kept_a, 2 * q + 2)
                pe.wait_ge(lv_kept, q + 1)
                for lev in range(1, 6):
                    for g in range(2):
                        pe.wait_ge(inv_ready, 12 * q + 2 * (lev - 1) + g + 1)
                        for i in range(3):
                            h = 3 * g + i
                            last = mm(bank[4 + g][:, i * P:(i + 1) * P], gram[0][:, h, :], inv[:, h, :])
                        last.then_inc(lt_done, 1)
                    n = 5 * tau + lev - 1
                    if 1 <= n <= HEADS:
                        times_v(l, n - 1)
                    if n < HEADS:
                        scores(l, n)
                    for g in range(2):
                        pe.wait_ge(lt_kept, 10 * q + 2 * (lev - 1) + g + 1)
                        for i in range(3):
                            h = 3 * g + i
                            last = mm(bank[g][:, i * P:(i + 1) * P], lt[:, h, :], invT[:, h, :])
                        if lev < 5:
                            for i in range(3):
                                h = 3 * g + i
                                last = mm(bank[6 + g][:, i * P:(i + 1) * P], invT[:, h, :], lt[:, h, :])
                        last.then_inc(tlt_done, 1)
                    if n < HEADS:
                        turn_probs(l, n)
                    if n == 9:
                        turn_output(l)
                pe.wait_ge(inv_ready, 12 * q + 12)
                for h in range(HEADS):
                    mm(bank[4][:, h * HD:(h + 1) * HD], invT[:, lane(h), :], lv[:, h * HD:(h + 1) * HD])
                for h in range(HEADS):
                    i = h // 2
                    last = mm(bank[6 + h % 2][:, i * P:(i + 1) * P], tok[0][:, i * P:(i + 1) * P], invT[:, lane(h), :])
                last.then_inc(p1_done, 1)
                if not tau:
                    pe.wait_ge(hs_sq, 2 * l + 2)
                    head_sum(3 * l + 2, conv_sq, 0)
                pe.wait_ge(p1_kept, q + 1)
                pe.wait_ge(ta_kept, q + 1)
                if not tau:
                    pe.wait_ge(state_zero, l + 1)
                for c in range(2):
                    ci = 2 * q + c
                    rows = slice(c * C, (c + 1) * C)
                    if ci:
                        pe.wait_ge(st_ready, ci)
                        pe.wait_ge(yc_kept, ci)
                    for i in range(NRT):
                        last = mm(bank[5][:, i * P:(i + 1) * P], ta_t[:, i, :], state[:, i, :])
                    last.then_inc(u_done, 1)
                    for i in range(NRT):
                        last = mm(bank[6][:, i * P:(i + 1) * P], rT[:, i, ts], state[:, i, :])
                    last.then_inc(yc_done, 1)
                    pe.wait_ge(u_ready, ci + 1)
                    for i in range(NRT):
                        cols = slice(i * P, (i + 1) * P)
                        mm(bank[7][:, cols], tok[1][rows, cols], u_tok[rows, cols], True, False)
                        last = mm(bank[7][:, cols], tok[2][rows, cols], tok[3][rows, cols], False, True)
                    last.then_inc(st_done, 1)
                for h in range(HEADS):
                    cols = slice(h * HD, (h + 1) * HD)
                    mm(bank[4][:, cols], gram[2][:, lane(h), :], u_tok[:, cols], True, False)
                    last = mm(bank[4][:, cols], gram[3][:, lane(h), :], tok[3][:, cols], False, True)
                last.then_inc(y_done, 1)
                if not tau:
                    head_spread(3 * l + 2, 2, (5,))
                    pe.wait_ge(yc_kept, 2 * q + 2)
                    pe.wait_ge(st_ready, 2 * q + 2)
                    token_major(1)
                else:
                    pe.wait_ge(hs_used, 3 * l + 3)
                    pe.wait_ge(att_out, l + 1)
                    out_weights(l, 0)
                    out_product(l, 0, OTHERS, True, False)
                    out_product(l, 1, OTHERS, True, False)
                pe.wait_ge(yn_ready, q + 1)
                for i in range(NRT):
                    last = pe.transpose(bank[5][:, i * P:(i + 1) * P], y_tok[:, i * P:(i + 1) * P], ident)
                last.then_inc(yt_done, 1)
                if tau:
                    out_product(l, 2, OTHERS, True, False)
                    out_product(l, 3, OTHERS, True, False)

            def scores(l, h):
                qT, kT = pT[:, 16:19, :], pT[:, 19:22, :]
                a = HEADS * l + h
                r = slice(h % 2 * HD, h % 2 * HD + HD)
                if h == 0:
                    pe.wait_ge(rope_ready, l + 1)
                mm(bank[2][:, 0:P], qT[r, h // 2, 0:P], kT[r, h // 2, 0:P])
                mm(bank[2][:, P:3 * P], qT[r, h // 2, P:T], kT[r, h // 2, :]).then_inc(sc_done, 1)

            def turn_probs(l, h):
                a = HEADS * l + h
                pe.wait_ge(ex_done, a + 1)
                for b in range(3):
                    last = pe.transpose(bank[3][:, b * P:(b + 1) * P], probs[a % 2][:, b * P:(b + 1) * P], ident)
                last.then_inc(tp_done, 1)

            def times_v(l, h):
                a = HEADS * l + h
                pe.wait_ge(tp_kept, a + 1)
                pe.wait_ge(sc_read, a + 1)
                if a:
                    pe.wait_ge(o_ready, a)
                cols = slice(h * HD, (h + 1) * HD)
                mm(bank[2][:, 384:448], probs_t[:, 0:P], v_att[:, 0, cols])
                mm(bank[2][:, 448:512], probs_t[:, P:2 * P], v_att[:, 0, cols], True, False)
                mm(bank[2][:, 448:512], probs_t[:, 2 * P:3 * P], v_att[:, 1, cols], False, True).then_inc(pv_done, 1)

            def turn_output(l):
                pe.wait_ge(on_ready, l + 1)
                for b in range(2):
                    for i in range(NRT):
                        last = pe.transpose(bank[2 + b][:, i * P:(i + 1) * P],
                                            o_tok[:, b, 2 * i:2 * i + 2, :].rearrange("p h d -> p (h d)"), ident)
                last.then_inc(ot_done, 1)

            for l in range(L):
                if l == 0:
                    norm(0)
                    pe.wait_ge(consts_in, 32)
                us = units(l)
                for u, unit in enumerate(us):
                    project(l, *unit, u)
                    at = unit[1:3]
                    if at == ("va", 0):
                        pe.wait_ge(qk_sq, l + 1)
                        head_sum(3 * l, [sq_qk[:, i, :] for i in range(6)], 4)
                    if at == ("vb", 0):
                        head_spread(3 * l, 6, (5, 6, 7))
                    if at == ("cm", 8):
                        pe.wait_ge(hs_used, 3 * l + 1)
                        for i in range(6):
                            last = mm(bank[5 + i // 2][:, i % 2 * T:i % 2 * T + T], const("rot"), pT[:, 16 + i, :])
                        last.then_inc(rot_done, 1)
                    if at == ("cm", 0):
                        pe.wait_ge(rope_ready, l + 1)
                        pe.wait_ge(lora_act, l + 1)
                        pe.wait_ge(inputs_in, 16 * N_INPUTS)
                        lora_product("w", l, (4, 5))
                        lora_product("a", l, (6, 7))
                    if at == ("cm", 2):
                        pe.wait_ge(lora_kept, LORA0[l] + 1)
                        lora_product("g", l, (4, 5))
                        if l:
                            pe.wait_ge(lora_kept, LORA0[l] + 2)
                            pe.wait_ge(vres_shifted, l)
                            lora_product("v", l, (6, 7))
                    if at == ("cm", 7):
                        pe.wait_ge(lora_kept, LORA0[l] + LORAS[l])
                        pe.wait_ge(hs_sq, 2 * l + 1)
                        head_sum(3 * l + 1, [tmp1[:, i, :] for i in range(NRT)], 4)
                    if at == ("cm", 13):
                        head_spread(3 * l + 1, 3, (5, 6))
                    if at == ("cm", 14):
                        pe.wait_ge(bonus_in, l + 1)
                        for i in range(NRT):
                            last = mm(bank[(4, 7)[i // 2]][:, i % 2 * T:i % 2 * T + T], const("pair"), tmp2[:, i, :])
                        last.then_inc(bonus_sum, 1)
                recurrence(l, 0)
                recurrence(l, 1)
                pe.wait_ge(y_out, 2 * l + 2)
                for m in range(KT):
                    if m >= 4:
                        if m == 4:
                            out_weights(l, 1)
                        pe.wait_ge(wo_added, 8 * l + m - 3)
                        out_product(l, m, OTHERS, True, False)
                    out_product(l, m, RWKV, False, True).then_inc(wo_done, 1)
                    if m:
                        sum_squares(2 * l + 1, m - 1)
                sum_squares(2 * l + 1, KT - 1)
                if l == 0:
                    def columns(kind, j):
                        if j:
                            pe.wait_ge(ds_done if kind == "g" else da_ready, j)
                        for q in range(4):
                            pe.wait_ge(lo_ready, DENSE0 + 4 * place_of[(kind, j)] + q + 1)
                            for i in range(2):
                                k = 2 * q + i
                                if kind == "g" and j == 0:
                                    pe.wait_ge(h_low, KT + k + 1)
                                for t in range(4):
                                    ws = slice(i * CW + t * P, i * CW + (t + 1) * P)
                                    last_ = three_w(bank[(0 if kind == "g" else 2) + t // 2][:, t % 2 * T:t % 2 * T + T],
                                                    w_hi[:, q, ws], w_lo[:, q, ws], h_hi[:, k, :], h_lo[:, k, :],
                                                    k == 0 and t % 2 == 0, k == KT - 1)
                            last_.then_inc(pc_free, 1)

                    def down(j):
                        pe.wait_ge(da_low, j + 1)
                        for q in range(4):
                            pe.wait_ge(lo_ready, DENSE0 + 4 * place_of[("d", j)] + q + 1)
                            for dt in range(KT):
                                ws = slice(dt * P, (dt + 1) * P)
                                last_ = three_w(bank[4 + dt // 2][:, dt % 2 * T:dt % 2 * T + T],
                                                w_hi[:, q, ws], w_lo[:, q, ws],
                                                da_parts(j)[0][:, q * T:(q + 1) * T],
                                                da_parts(j)[1][:, q * T:(q + 1) * T], j == 0 and q == 0 and dt % 2 == 0,
                                                j == NJ - 1 and q == 3)
                            last_.then_inc(pc_free, 1)

                    def three_w(*a):
                        return three(*a, skip_group_check=True)

                    for kind, j in ORDER:
                        if kind == "d":
                            down(j)
                        else:
                            columns(kind, j)
                    norm(2)

            for b in range(2):
                for k in range(KT):
                    if b == 0:
                        pe.wait_ge(h_ready, KT * (2 * L - 1) + k + 1)
                    last = mm(bank[0][:, b * NE:(b + 1) * NE], hT[:, k, b * P:(b + 1) * P], router_w[:, k, :],
                              k == 0, k == KT - 1)
            last.then_inc(logit_done, 1)
            for f in range(8):
                src, b, hf = (hT, xT)[f // 4], f // 2 % 2, f % 2
                if f >= 4:
                    pe.wait_ge(act_turned, f - 3)
                for i in range(4):
                    last = pe.transpose(bank[4 + f % 4][:, i * P:(i + 1) * P], src[:, 4 * hf + i, b * P:(b + 1) * P],
                                        ident)
                last.then_inc(pe_turned, 1)
            sel = small[:, 0:16]
            pe.wait_ge(route_sel, 1)
            mm(bank[1][:, 0:8], const("tri"), sel[:, 0:8])
            mm(bank[1][:, 8:16], const("tri"), sel[:, 8:16], True, False)
            mm(bank[1][:, 8:16], ones, sel[:, 0:8], False, True)
            mm(bank[1][:, 16:24], ones, sel[:, 0:8], True, False)
            mm(bank[1][:, 16:24], ones, sel[:, 8:16], False, True).then_inc(rank_done, 1)

            def moe_pass(p):
                def turn_combine():
                    pe.wait_ge(gated_ready, p + 1)
                    pe.wait_ge(act_turned, 8)
                    for f in range(4):
                        if f >= 2:
                            pe.wait_ge(cb_kept, 4 * p + f - 1)
                        for i in range(2):
                            for b in range(2):
                                c0 = i * T + b * P
                                last_ = pe.transpose(bank[6 + f % 2][:, c0:c0 + P], gated[:, b, 2 * f + i, :], ident)
                        last_.then_inc(cb_done, 1)

                def gather(e, at1):
                    for f in range(2):
                        for i in range(4):
                            k = 4 * f + i
                            for b in range(2):
                                last_ = mm(bank[1 + 2 * f][:, i * P:(i + 1) * P], h_tok[:, b, k * P:(k + 1) * P],
                                           onehot[:, b, e, :], b == 0, b == 1)
                        last_.then_inc(ga_done, 1)

                def column_chunk(kind, j, at1):
                    if j >= 2:
                        pe.wait_ge(ac_ready, at1 * NJ + (j - 1))
                    b = bank[(0 if kind == "g" else 2) + j % 2]
                    for q in range(4):
                        pe.wait_ge(lo_ready, at1 * PIECES_E + (MOE0 + 4 * place_of[(kind, j)] + q + 1))
                        for i in range(2):
                            k = 2 * q + i
                            ks, cs = slice(k * P, (k + 1) * P), slice(i * CW, (i + 1) * CW)
                            last_ = three(b[:, :], xg_hi[:, ks], xg_lo[:, ks], w_hi[:, q, cs], w_lo[:, q, cs],
                                          k == 0, k == KT - 1)
                        last_.then_inc(pc_free, 1)

                def turn(j, at1):
                    pe.wait_ge(ac_ready, at1 * NJ + (j + 1))
                    if j:
                        pe.wait_ge(at_low, at1 * NJ + j)
                    else:
                        pe.wait_ge(cbe_ready, at1 + 1)
                    for i in range(4):
                        last_ = pe.transpose(bank[6][:, i * P:(i + 1) * P], act_b[j % 2][:, i * P:(i + 1) * P],
                                             ident)
                    last_.then_inc(at_done, 1)

                def down(j, at1):
                    pe.wait_ge(at_low, at1 * NJ + (j + 1))
                    for q in range(4):
                        pe.wait_ge(lo_ready, at1 * PIECES_E + (MOE0 + 4 * place_of[("d", j)] + q + 1))
                        for hf in range(2):
                            ks, cs = slice(q * P, (q + 1) * P), slice(hf * CW, (hf + 1) * CW)
                            last_ = three(bank[4 + hf][:, :], at_hi[:, j % 2, ks], at_lo[:, j % 2, ks],
                                          w_hi[:, q, cs], w_lo[:, q, cs], j == 0 and q == 0, j == NJ - 1 and q == 3)
                        last_.then_inc(pc_free, 1)

                def scatter(at1):
                    pe.wait_ge(yg_kept, at1 * 2 + 2)
                    pe.wait_ge(cbe_ready, at1 + 1)
                    for f in range(4):
                        b, hf = f // 2, f % 2
                        mm(bank[(6, 7, 4, 5)[f]][:, :], combine_e[:, b * P:(b + 1) * P],
                           yg[:, hf * 512:(hf + 1) * 512]).then_inc(sct_done, 1)

                def expert(e, at1, last_one):
                    for j in range(1, NJ):
                        column_chunk("g", j, at1)
                        turn(j - 1, at1)
                        column_chunk("u", j, at1)
                        down(j - 1, at1)
                    turn(NJ - 1, at1)
                    if not last_one:
                        gather(e + 1, at1 + 1)
                    down(NJ - 1, at1)
                    if not last_one:
                        pe.wait_ge(ga_low, at1 * 2 + 4)
                        column_chunk("g", 0, at1 + 1)
                    scatter(at1)
                    if not last_one:
                        column_chunk("u", 0, at1 + 1)

                first = p * NE
                pe.wait_ge(oh_ready, p + 1)
                if p == 0:
                    pe.wait_ge(act_turned, 4)
                gather(0, first)
                pe.wait_ge(ga_low, first * 2 + 2)
                column_chunk("g", 0, first)
                turn_combine()
                column_chunk("u", 0, first)
                with pe.Fori(0, NE - 1) as e:
                    expert(e, e + first, False)
                expert(NE - 1, first + NE - 1, True)

            moe_pass(0)
            pe.wait_ge(flag_ready, 1)
            over_full = pe.value_load(flag[0:1, 0:1])
            with pe.If(over_full > 0):
                moe_pass(1)

        @block.scalar
        def _(act):
            steps = [0]

            def then(ins):
                steps[0] += 1
                ins.then_inc(act_step, 1)
                act.wait_ge(act_step, steps[0])

            def copy(o, i, **kw):
                return act.activation(o, i, ACT.Copy, **kw)

            act.dma_start(mask_in, masks).then_inc(inputs_in, 16)
            act.dma_start(lora_w, lora.rearrange("l p n -> p l n")).then_inc(inputs_in, 16)
            act.dma_start(v2w[0:16, :], vres_v2).then_inc(inputs_in, 16)
            act.dma_start(vres_wt, vres_w.rearrange("(k p) n -> p k n", p=P)).then_inc(inputs_in, 16)
            act.dma_start(router_w, router.rearrange("(k p) n -> p k n", p=P)).then_inc(inputs_in, 16)
            for i in range(4):
                act.wait_ge(x_turned, i + 1)
                copy(xT[:, 2 * i:2 * i + 2, :].rearrange("p k t -> p (k t)"), bank[i][:, :]).then_inc(x_kept, 1)

            def high_h(n):
                for k in range(KT):
                    act.wait_ge(h_ready, KT * n + k + 1)
                    copy(h_hi[:, k, :], hT[:, k, :]).then_inc(h_high, 1)

            def split_in(l, ch):
                for q in range(4):
                    n = halves[("in", l, ch, q // 2)]
                    if q % 2 == 0:
                        act.wait_ge(ring_in[slot_of[n]], count_of[n])
                    copy(w_hi[:, q, :], ring[:, slot_of[n], q % 2 * PIECE:(q % 2 + 1) * PIECE]).then_inc(hi_ready, 1)

            def norm(n, ready, between=None):
                done, base, tiles = ready
                for i in range(KT // tiles):
                    act.wait_ge(done, base + i + 1)
                    ks = slice(tiles * i, tiles * (i + 1))
                    act.activation(hT[:, ks, :], xT[:, ks, :], ACT.Square).then_inc(sq_ready, tiles)
                    if between and i == KT // tiles // 2:
                        between()
                act.wait_ge(ms_ready, n + 1)
                act.activation(rn, rn, ACT.Sqrt).then_inc(rn_ready, 1)

            def root(n):
                act.wait_ge(hs_rec, n + 1)
                act.activation(head_rn[0:SEL_ROWS, :], head_rn[0:SEL_ROWS, :], ACT.Sqrt).then_inc(hs_root, 1)

            def keep_unit(l, u, kind, n):
                g = UNIT0[l] + u
                act.wait_ge(unit_done, g + 1)
                b = bank[g % 4]
                if kind == "cm":
                    ins = copy(pT[:, n, :], b[:, 0:T])
                elif kind == "vres":
                    ins = copy(pv[0:16, :], b[0:16, 0:T])
                elif kind == "va":
                    ins = copy(v_att[:, n, 0:2 * P], b[:, 0:2 * P])
                else:
                    ins = copy(v_att[:, n, 2 * P:3 * P], b[:, 0:P])
                ins.then_inc(unit_kept, 1)

            def keep_lora(l, n, o, banks, func, bias):
                act.wait_ge(lora_done, LORA0[l] + n + 1)
                for i in range(NRT):
                    src = bank[banks[i // 2]][:, i % 2 * T:i % 2 * T + T]
                    if bias:
                        last = act.activation(o[:, i, :], src, func, bias=param(l, bias, i))
                    else:
                        last = copy(o[:, i, :], src)
                last.then_inc(lora_kept, 1)

            def recurrence(l, tau):
                q = 2 * l + tau
                for n in range(2):
                    act.wait_ge(tok_done, 4 * q + n + 1)
                    copy(tok[n], bank[TOK_BANKS[n]][:, 0:RW]).then_inc(tok_kept_a, 1)
                act.wait_ge(lv_done, q + 1)
                copy(lv, bank[6][:, 0:RW]).then_inc(lv_kept, 1)
                for lev in range(1, 6):
                    for g in range(2):
                        act.wait_ge(lt_done, 10 * q + 2 * (lev - 1) + g + 1)
                        copy(lt[:, 3 * g:3 * g + 3, :].rearrange("p h t -> p (h t)"), bank[4 + g][:, 0:3 * P]).then_inc(
                            lt_kept, 1)
                    n = 5 * tau + lev - 1
                    if n < HEADS:
                        exponentials(l, n)
                    if n == 8:
                        act.wait_ge(on_rec, l + 1)
                        act.activation(small[:, 96:108], small[:, 96:108], ACT.Sqrt).then_inc(on_root, 1)
                act.wait_ge(p1_done, q + 1)
                copy(p1, bank[4][:, 0:RW])
                copy(ta_t[0:HD, :, :].rearrange("p i t -> p (i t)"), bank[6][0:HD, 0:RW]).then_inc(p1_kept, 1)
                for c in range(2):
                    rows = slice(c * C, (c + 1) * C)
                    act.wait_ge(yc_done, 2 * q + c + 1)
                    copy(y_cross[rows, :], bank[6][rows, 0:RW]).then_inc(yc_kept, 1)
                if not tau:
                    root(3 * l + 2)
                act.wait_ge(gn_rec, q + 1)
                act.activation(small[:, 64:70], small[:, 64:70], ACT.Sqrt).then_inc(gn_root, 1)

            def exponentials(l, h):
                a = HEADS * l + h
                act.wait_ge(mx_ready, a + 1)
                for b, cols in enumerate((slice(0, P), slice(P, 3 * P))):
                    pr = probs[a % 2][:, cols]
                    at_ = 2 * (a % 2) + b
                    last = act.activation(pr, pr, ACT.Exp, bias=small[:, 80 + at_:81 + at_],
                                          accum_out=small[:, 84 + at_:85 + at_])
                last.then_inc(ex_done, 1)
                act.wait_ge(tp_done, a + 1)
                copy(probs_t, bank[3][:, 0:3 * P]).then_inc(tp_kept, 1)

            def dense_split(kind, j):
                for q in range(4):
                    n = halves[(kind, 0, j, q // 2)]
                    if q % 2 == 0:
                        act.wait_ge(ring_in[slot_of[n]], count_of[n])
                    act.wait_ge(pc_free, 4 * place_of[(kind, j)] + q + 1)
                    copy(w_hi[:, q, :], ring[:, slot_of[n], q % 2 * PIECE:(q % 2 + 1) * PIECE]).then_inc(
                        hi_ready, 1)

            def split(kind, j, at1, pieces=range(4)):
                for q in pieces:
                    c = 4 * place_of[(kind, j)] + q
                    h = c // 2
                    if q % 2 == 0:
                        act.wait_ge(ring_in[e_slot[h]], at1 * (16 * FILLS) + e_count[h])
                    act.wait_ge(pc_free, at1 * PIECES_E + (PIECES_E + c + 1))
                    raw = ring[:, e_slot[h], c % 2 * PIECE:(c % 2 + 1) * PIECE]
                    copy(w_hi[:, q, :], raw).then_inc(hi_ready, 1)

            for l in range(L):
                norm(2 * l, (x_ffn, 0, 2) if l else (x_kept, 0, 2))
                high_h(2 * l)
                us = units(l)
                for u, (_, kind, n, _, _) in enumerate(us):
                    keep_unit(l, u, kind, n)
                    if (kind, n) == ("cm", 21):
                        act.wait_ge(unit_kept, kept(l, "cm", 21))
                        act.activation(sq_qk, pT[:, 16:22, :], ACT.Square).then_inc(qk_sq, 1)
                    if (kind, n) == ("va", 1):
                        root(3 * l)
                        split_in(l, 2)
                    if (kind, n) == ("cm", 11):
                        act.wait_ge(lora_ready, l + 1)
                        act.activation(lora_in[0:32, :], lora_in[0:32, :], ACT.Tanh)
                        act.activation(lora_in[64:128, :], lora_in[64:128, :], ACT.Sigmoid).then_inc(lora_act, 1)
                        split_in(l, 1)
                    if (kind, n) == ("cm", 1):
                        act.wait_ge(consts_in, 32)
                        keep_lora(l, 0, sig_w, (4, 5), ACT.Sigmoid, "w0")
                        keep_lora(l, 1, a_gate, (6, 7), ACT.Sigmoid, "a0")
                    if (kind, n) == ("cm", 3):
                        keep_lora(l, 2, g_gate, (4, 5), ACT.Copy, None)
                        if l:
                            keep_lora(l, 3, bonus, (6, 7), ACT.Sigmoid, "vres_v0")
                    if (kind, n) == ("cm", 5):
                        act.wait_ge(cs_ready, l + 1)
                        then(act.activation(inv_w.rearrange("p i (c t) -> p i c t", c=NC), w65[:, :, :, 1:C + 1],
                                            ACT.Exp, scale=DECAY))
                        act.activation(w65, w65, ACT.Exp, scale=-DECAY).then_inc(w_ready, 1)
                    if (kind, n) == ("cm", 12):
                        root(3 * l + 1)
                recurrence(l, 0)
                recurrence(l, 1)
                norm(2 * l + 1, (wo_added, 8 * l, 1), lambda: split("g", 0, 0) if l else dense_split("g", 0))
                if l == 0:
                    high_h(1)
                if l == 0:

                    def dense_silu(j):
                        act.wait_ge(pc_free, PIECES + 4 * (place_of[("g", j)] + 1))
                        if j:
                            act.wait_ge(da_ready, j)
                        for i in range(2):
                            last = act.activation(dense_sil[:, i * 512:(i + 1) * 512], bank[i][:, :], ACT.Silu)
                        last.then_inc(ds_done, 1)

                    def dense_high(j):
                        act.wait_ge(da_ready, j + 1)
                        if j:
                            last_user = ("d", j - 1) if j < NJ - 1 else ("u", j)
                            act.wait_ge(pc_free, PIECES + 4 * (place_of[last_user] + 1))
                        copy(da_parts(j)[0], dense_act).then_inc(da_high, 1)

                    dense_split("u", 0)
                    dense_silu(0)
                    for j in range(1, NJ):
                        dense_split("g", j)
                        dense_high(j - 1)
                        dense_split("u", j)
                        dense_silu(j)
                        dense_split("d", j - 1)
                    dense_high(NJ - 1)
                    dense_split("d", NJ - 1)

            for f in range(8):
                dst, b, hf = (h_tok, x_tok)[f // 4], f // 2 % 2, f % 2
                act.wait_ge(pe_turned, f + 1)
                copy(dst[:, b, 512 * hf:512 * (hf + 1)], bank[4 + f % 4][:, :]).then_inc(act_turned, 1)
                if f == 3:
                    act.wait_ge(route_act, 1)
                    act.activation(top_gap, top_gap, ACT.Exp).then_inc(route_exp, 1)

            def moe_pass(p):
                def gathered(at1):
                    for f in range(2):
                        act.wait_ge(ga_done, at1 * 2 + (f + 1))
                        copy(xg_hi[:, f * CW:(f + 1) * CW], bank[1 + 2 * f][:, :]).then_inc(ga_kept, 1)

                def silu(j, at1):
                    act.wait_ge(pc_free, at1 * PIECES_E + (PIECES_E + 4 * (place_of[("g", j)] + 1) + PIECES))
                    if j >= 2:
                        act.wait_ge(ac_ready, at1 * NJ + (j - 1))
                    act.activation(sil_b[j % 2], bank[j % 2][:, :], ACT.Silu).then_inc(sl_done, 1)

                def turned(j, at1):
                    act.wait_ge(at_done, at1 * NJ + (j + 1))
                    copy(at_hi[:, j % 2, :], bank[6][:, :]).then_inc(at_kept, 1)

                def expert(e, at1, last_one):
                    for j in range(1, NJ):
                        split("g", j, at1)
                        split("u", j, at1)
                        turned(j - 1, at1)
                        silu(j, at1)
                        split("d", j - 1, at1)
                    split("d", NJ - 1, at1, range(0, TURN_AT))
                    turned(NJ - 1, at1)
                    split("d", NJ - 1, at1, range(TURN_AT, 4))
                    if not last_one:
                        gathered(at1 + 1)
                        split("g", 0, at1 + 1)
                    act.wait_ge(pc_free, at1 * PIECES_E + (2 * PIECES_E + PIECES))
                    for hf in range(2):
                        copy(yg[:, hf * 512:(hf + 1) * 512], bank[4 + hf][:, :]).then_inc(yg_kept, 1)
                    if not last_one:
                        split("u", 0, at1 + 1)
                        silu(0, at1 + 1)

                first = p * NE
                gathered(first)
                if p:
                    split("g", 0, first)
                split("u", 0, first)
                for f in range(4):
                    act.wait_ge(cb_done, 4 * p + f + 1)
                    copy(combine[:, 2 * f:2 * f + 2, :].rearrange("p e t -> p (e t)"), bank[6 + f % 2][:, :]).then_inc(
                        cb_kept, 1)
                silu(0, first)
                with act.Fori(0, NE - 1) as e:
                    expert(e, e + first, False)
                expert(NE - 1, first + NE - 1, True)

            moe_pass(0)
            act.wait_ge(flag_ready, 1)
            over_full = act.value_load(flag[0:1, 0:1])
            with act.If(over_full > 0):
                moe_pass(1)
            act.wait_ge(moe_done, 1)
            act.dma_start(out.rearrange("(b p) d -> p b d", p=P), x_tok).then_inc(out_done, 16)
            act.wait_ge(out_done, 16)

        @block.vector
        def _(dve):
            steps = [0]

            def then(ins):
                steps[0] += 1
                ins.then_inc(dve_step, 1)
                dve.wait_ge(dve_step, steps[0])

            TT = dve.tensor_tensor
            TS = dve.tensor_scalar
            STT = dve.scalar_tensor_tensor

            def split_in(l, ch):
                for q in range(4):
                    n = halves[("in", l, ch, q // 2)]
                    dve.wait_ge(hi_ready, IN0[l, ch] + q + 1)
                    TT(w_lo[:, q, :], ring[:, slot_of[n], q % 2 * PIECE:(q % 2 + 1) * PIECE],
                       w_hi[:, q, :].bitcast(F32), ALU.subtract).then_inc(lo_ready, 1)

            def h_low_part(n, k):
                dve.wait_ge(h_high, KT * n + k + 1)
                TT(h_lo[:, k, :], hT[:, k, :], h_hi[:, k, :].bitcast(F32), ALU.subtract).then_inc(h_low, 1)

            def norm(n, l, gain):
                dve.wait_ge(ss_ready, n + 1)
                then(TS(rn, bank[SUM_BANKS[n]][:, 0:T], 1.0 / D, NORM_EPS, ALU.mult, ALU.add))
                dve.reciprocal(rn, rn).then_inc(ms_ready, 1)
                if n == 0:
                    dve.wait_ge(inputs_in, 16 * N_INPUTS)
                    then(dve.tensor_copy(mask8[:, :], mask_in))
                dve.wait_ge(rn_ready, n + 1)
                for k in range(KT):
                    STT(hT[:, k, :], xT[:, k, :], param(l, gain, k), rn, ALU.mult, ALU.mult).then_inc(h_ready, 1)
                    if n == 1 and k:
                        h_low_part(n, k - 1)
                if n == 1:
                    h_low_part(n, KT - 1)
                dve.wait_ge(h_ready, KT * (n + 1))

            def shift(l, p_, mu, t_, o_=None, rows=P):
                n = p_.shape[1]
                t_ = t_[:, 0:n, :]
                then(TS(t_[0:rows, :, 0:1], p_[0:rows, :, 0:1], -1.0, None, ALU.mult))
                then(TT(t_[0:rows, :, 1:T], p_[0:rows, :, 0:T - 1], p_[0:rows, :, 1:T], ALU.subtract))
                for i in range(n):
                    o = p_[0:rows, i, :] if o_ is None else o_
                    ins = STT(o, t_[0:rows, i, :], mu(i)[0:rows, :], p_[0:rows, i, :], ALU.mult, ALU.add)
                return ins

            def head_factor(n, b, first, second, ops):
                dve.wait_ge(hs_sum, n + 1)
                then(TS(head_rn[0:SEL_ROWS, :], bank[b][0:SEL_ROWS, 0:T], first, second, *ops))
                dve.reciprocal(head_rn[0:SEL_ROWS, :], head_rn[0:SEL_ROWS, :]).then_inc(hs_rec, 1)

            def recurrence(l, tau):
                q = 2 * l + tau
                for n in (2, 3):
                    dve.wait_ge(tok_done, 4 * q + n + 1)
                    TS(tok[n], bank[TOK_BANKS[n]][:, 0:RW], 1.0, None, ALU.mult).then_inc(tok_kept_d, 1)
                strict = spread(const("strict"), 3)
                incl = spread(const("incl"), 3)

                def as3(b):
                    return bank[b][:, 0:3 * P].rearrange("p (i t) -> p i t", i=3)

                def keep_gram(n, g_, mask, b0):
                    dve.wait_ge(gram_done, 5 * q + n + 1)
                    for g in range(2):
                        last = TT(gram[g_][:, 3 * g:3 * g + 3, :], as3(b0 + g), mask, ALU.mult)
                    last.then_inc(gram_kept, 1)

                dve.wait_ge(inv_init, 2 * q + 2)
                dve.wait_ge(gram_done, 5 * q + 1)
                for g in range(2):
                    then(dve.copy_predicated(invT[:, 3 * g:3 * g + 3, :], spread(lmask[:, 1, 0, :], 3), as3(4 + g)))
                keep_gram(0, 0, strict, 4)
                dve.wait_ge(gram_done, 5 * q + 2)
                for g in range(2):
                    dve.copy_predicated(inv[:, 3 * g:3 * g + 3, :], spread(lmask[:, 0, 0, :], 3), as3(6 + g)).then_inc(
                        inv_ready, 1)
                keep_gram(2, 1, strict, 4)
                keep_gram(3, 2, incl, 6)
                keep_gram(4, 3, incl, 4)
                for lev in range(1, 6):
                    n = 5 * tau + lev - 1
                    if n < HEADS:
                        largest_score(l, n)
                    for g in range(2):
                        hs = slice(3 * g, 3 * g + 3)
                        dve.wait_ge(tlt_done, 10 * q + 2 * (lev - 1) + g + 1)
                        last = dve.copy_predicated(invT[:, hs, :], spread(lmask[:, 1, lev, :], 3), as3(g))
                        if lev < 5:
                            then(last)
                            last = dve.copy_predicated(inv[:, hs, :], spread(lmask[:, 0, lev, :], 3), as3(6 + g))
                        last.then_inc(inv_ready, 1)
                    if 1 <= n <= HEADS:
                        keep_output(l, n - 1)
                    if n == HEADS + 1:
                        output_squares(l)
                    if n == HEADS + 2:
                        dve.wait_ge(on_root, l + 1)
                        TT(o12, o12, stretch(out_ss, HD), ALU.mult).then_inc(on_ready, 1)
                dve.wait_ge(p1_done, q + 1)
                TS(ta_t[HD:P, :, :].rearrange("p i t -> p (i t)"), bank[7][HD:P, 0:RW], 1.0, None, ALU.mult).then_inc(
                    ta_kept, 1)
                dve.wait_ge(p1_kept, q + 1)
                for c in range(2):
                    ci = 2 * q + c
                    rows = slice(c * C, (c + 1) * C)
                    chunk = 2 * tau + c
                    then(TT(end_w, spread(const("pair"), NRT),
                            w65[:, :, chunk, C:C + 1].to_broadcast([P, NRT, P]), ALU.mult))
                    dve.wait_ge(u_done, ci + 1)
                    TT(u_tok[rows, :], bank[5][rows, 0:RW], p1[rows, :], ALU.add).then_inc(u_ready, 1)
                    dve.wait_ge(st_done, ci + 1)
                    then(TT(state_tmp, bank[7][:, 0:RW].rearrange("p (i v) -> p i v", i=NRT), state, ALU.add))
                    TT(state, state_tmp, end_w, ALU.mult).then_inc(st_ready, 1)
                    dve.wait_ge(st_ready, ci + 1)
                if tau:
                    dve.wait_ge(ot_done, l + 1)
                    for b in range(2):
                        for i in range(NRT):
                            last = TS(pT[:, 16 + i, b * P:(b + 1) * P], bank[2 + b][:, i * P:(i + 1) * P],
                                      param(l, "out_g", i), None, ALU.mult)
                    last.then_inc(att_out, 1)
                else:
                    head_factor(3 * l + 2, 0, 1.0 / HD, NORM_EPS, (ALU.mult, ALU.add))
                y3 = y_tok.rearrange("p (h d) -> p h d", h=HEADS)
                dve.wait_ge(y_done, q + 1)
                dve.wait_ge(yc_kept, 2 * q + 2)
                then(TT(y_tok, bank[4][:, 0:RW], y_cross, ALU.add))
                mean, var = small[:, 70:76], small[:, 64:70]
                then(dve.tensor_reduce(mean, y3, AX.X, ALU.add))
                then(TS(mean, mean, 1.0 / HD, None, ALU.mult))
                then(TT(y3, y3, stretch(mean, HD), ALU.subtract))
                sq3 = y_cross.rearrange("p (h d) -> p h d", h=HEADS)
                then(TT(sq3, y3, y3, ALU.mult))
                then(dve.tensor_reduce(var, sq3, AX.X, ALU.add))
                then(TS(var, var, 1.0 / HD, GN_EPS, ALU.mult, ALU.add))
                dve.reciprocal(var, var).then_inc(gn_rec, 1)
                if not tau:
                    dve.wait_ge(hs_bc, 3 * l + 3)
                    for i in range(2):
                        last = STT(pT[:, 10 + i, :], pT[:, 12 + i, :], param(l, "conv_g", i),
                                   bank[5][:, i * T:(i + 1) * T], ALU.mult, ALU.mult)
                    last.then_inc(hs_used, 1)
                dve.wait_ge(gn_root, q + 1)
                TT(y3, y3, stretch(var, HD), ALU.mult).then_inc(yn_ready, 1)
                dve.wait_ge(yt_done, q + 1)
                ts = slice(tau * P, (tau + 1) * P)
                for i in range(NRT):
                    last = TS(pT[:, i, ts], bank[5][:, i * P:(i + 1) * P], param(l, "ln_w", i), param(l, "ln_b", i),
                              ALU.mult, ALU.add)
                then(last)
                then(TT(pT[:, 0:3, ts], pT[:, 0:3, ts], bonus[:, :, ts], ALU.add))
                TT(pT[:, 0:3, ts], pT[:, 0:3, ts], g_gate[:, :, ts], ALU.mult).then_inc(y_out, 1)
                dve.wait_ge(y_out, q + 1)

            def largest_score(l, h):
                a = HEADS * l + h
                pr = probs[a % 2]
                nmax = small[:, 80 + 2 * (a % 2):82 + 2 * (a % 2)]
                dve.wait_ge(sc_done, a + 1)
                if a >= 2:
                    dve.wait_ge(tp_done, a - 1)
                STT(pr, bank[2][:, 0:3 * P], HD ** -0.5, const("bias"), ALU.mult, ALU.add).then_inc(sc_read, 1)
                dve.wait_ge(sc_read, a + 1)
                dve.tensor_reduce(nmax[:, 0:1], pr[:, 0:P], AX.X, ALU.max)
                then(dve.tensor_reduce(nmax[:, 1:2], pr[:, P:3 * P], AX.X, ALU.max))
                TS(nmax, nmax, -1.0, None, ALU.mult).then_inc(mx_ready, 1)

            def keep_output(l, h):
                a = HEADS * l + h
                at_ = 2 * (a % 2)
                dve.wait_ge(ex_done, a + 1)
                then(dve.reciprocal(small[:, 88 + at_:90 + at_], small[:, 84 + at_:86 + at_]))
                dve.wait_ge(pv_done, a + 1)
                for b in range(2):
                    last = TS(o_tok[:, b, h, :], bank[2][:, 384 + b * HD:384 + (b + 1) * HD],
                              small[:, 88 + at_ + b:89 + at_ + b], None, ALU.mult)
                last.then_inc(o_ready, 1)
                dve.wait_ge(o_ready, a + 1)

            out_ss = small[:, 96:108]
            o12 = o_tok.rearrange("p b h d -> p (b h) d")

            def output_squares(l):
                s12 = o_sq.rearrange("p b h d -> p (b h) d")
                then(TT(s12, o12, o12, ALU.mult))
                then(dve.tensor_reduce(out_ss, s12, AX.X, ALU.add))
                then(TS(out_ss, out_ss, 1.0 / HD, NORM_EPS, ALU.mult, ALU.add))
                dve.reciprocal(out_ss, out_ss).then_inc(on_rec, 1)

            def dense_split(kind, j):
                for q in range(4):
                    n = halves[(kind, 0, j, q // 2)]
                    dve.wait_ge(hi_ready, DENSE0 + 4 * place_of[(kind, j)] + q + 1)
                    TT(w_lo[:, q, :], ring[:, slot_of[n], q % 2 * PIECE:(q % 2 + 1) * PIECE],
                       w_hi[:, q, :].bitcast(F32), ALU.subtract).then_inc(lo_ready, 1)

            def split(kind, j, at1, pieces=range(4)):
                for q in pieces:
                    c = 4 * place_of[(kind, j)] + q
                    dve.wait_ge(hi_ready, at1 * PIECES_E + (MOE0 + c + 1))
                    raw = ring[:, e_slot[c // 2], c % 2 * PIECE:(c % 2 + 1) * PIECE]
                    TT(w_lo[:, q, :], raw, w_hi[:, q, :].bitcast(F32), ALU.subtract).then_inc(lo_ready, 1)

            dve.wait_ge(ident_in, 16)
            dve.wait_ge(consts_in, 32)
            for l in range(L):
                norm(2 * l, l, "mix_norm")
                rT, kT, vT = pT[:, 0:3, :], pT[:, 3:6, :], pT[:, 6:9, :]
                for k in range(KT):
                    h_low_part(2 * l, k)
                head_factor(3 * l, 4, 1.0 / HD, NORM_EPS, (ALU.mult, ALU.add))
                split_in(l, 2)
                dve.wait_ge(hs_bc, 3 * l + 1)
                for i in range(6):
                    last = STT(pT[:, 16 + i, :], pT[:, 16 + i, :], param(l, "q_g" if i < 3 else "k_g"),
                               bank[5 + i // 2][:, i % 2 * T:i % 2 * T + T], ALU.mult, ALU.mult)
                last.then_inc(hs_used, 1)
                dve.wait_ge(rot_done, l + 1)
                for i in range(3):
                    TT(sq_qk[:, 2 * i:2 * i + 2, :], bank[5 + i][:, :].rearrange("p (i t) -> p i t", i=2),
                       spread(const("sin"), 2), ALU.mult)
                qk = pT[:, 16:22, :]
                then(TT(qk, qk, spread(const("cos"), 6), ALU.mult))
                TT(qk, qk, sq_qk, ALU.add).then_inc(rope_ready, 1)
                dve.wait_ge(unit_kept, kept(l, "cm", 9))
                shift(l, pT[:, 9:10, :], lambda i: param(l, "mu", 9), tmp1, lora_in).then_inc(lora_ready, 1)
                dve.wait_ge(lora_ready, l + 1)
                if l:
                    dve.wait_ge(unit_kept, kept(l, "vres", 0))
                    pv3 = pv.rearrange("p (a t) -> p a t", a=1)
                    shift(l, pv3, lambda i: param(l, "vres_mu"), tmp1, None, 16).then_inc(vres_shifted, 1)
                    dve.wait_ge(vres_shifted, l)
                split_in(l, 1)
                dve.wait_ge(unit_kept, kept(l, "cm", 2))
                then(shift(l, rT, lambda i: param(l, "mu", i), tmp1))
                dve.memset(w65[:, :, :, 0:1], 0.0)
                dve.wait_ge(lora_kept, LORA0[l] + 1)
                for i in range(NRT):
                    for c in range(NC):
                        last = dve.tensor_tensor_scan(w65[:, i, c, 1:C + 1], const("ones")[:, 0:C],
                                                      sig_w[:, i, c * C:(c + 1) * C], 0.0, ALU.mult, ALU.add)
                last.then_inc(cs_ready, 1)
                dve.wait_ge(unit_kept, kept(l, "cm", 5))
                then(shift(l, kT, lambda i: param(l, "mu", 3 + i), tmp1))
                for i in range(NRT):
                    last = TS(kk[:, i, :], kT[:, i, :], param(l, "k_k", i), None, ALU.mult)
                then(last)
                TT(tmp1, kk, kk, ALU.mult).then_inc(hs_sq, 1)
                dve.wait_ge(lora_kept, LORA0[l] + 2)
                for i in range(NRT):
                    last = TS(tmp2[:, i, :], a_gate[:, i, :], 1.0, param(l, "k_a", i), ALU.subtract, ALU.mult)
                then(last)
                for i in range(NRT):
                    last = STT(kT[:, i, :], tmp2[:, i, :], 1.0, kT[:, i, :], ALU.add, ALU.mult)
                then(last)
                for i in range(NRT):
                    last = STT(tmp2[:, i, :], rT[:, i, :], param(l, "r_k", i), kT[:, i, :], ALU.mult, ALU.mult)
                last.then_inc(bonus_in, 1)
                dve.wait_ge(bonus_in, l + 1)
                dve.wait_ge(w_ready, l + 1)
                TT(kT, kT, inv_w, ALU.mult)
                TT(rT.rearrange("p i (c t) -> p i c t", c=NC), rT.rearrange("p i (c t) -> p i c t", c=NC),
                   w65[:, :, :, 1:C + 1], ALU.mult)
                dve.wait_ge(hs_sum, 3 * l + 2)
                then(TS(head_rn[0:SEL_ROWS, :], bank[4][0:SEL_ROWS, 0:T], 1e-24, None, ALU.max))
                dve.reciprocal(head_rn[0:SEL_ROWS, :], head_rn[0:SEL_ROWS, :]).then_inc(hs_rec, 1)
                dve.wait_ge(unit_kept, kept(l, "cm", 7))
                then(shift(l, vT, lambda i: param(l, "mu", 6 + i), tmp1))
                if l == 0:
                    then(TS(v_first, vT, 1.0, None, ALU.mult))
                else:
                    dve.wait_ge(lora_kept, LORA0[l] + 4)
                    then(TT(tmp1, v_first, vT, ALU.subtract))
                    then(TT(tmp1, tmp1, bonus, ALU.mult))
                    then(TT(vT, vT, tmp1, ALU.add))
                dve.wait_ge(hs_bc, 3 * l + 2)
                TT(kk[:, 0:2, :], kk[:, 0:2, :], bank[5][:, :].rearrange("p (i t) -> p i t", i=2), ALU.mult)
                TT(kk[:, 2, :], kk[:, 2, :], bank[6][:, 0:T], ALU.mult).then_inc(hs_used, 1)
                dve.wait_ge(hs_used, 3 * l + 2)
                then(TT(a_gate, kk, a_gate, ALU.mult))
                dve.wait_ge(bonus_sum, l + 1)
                TT(bonus[:, 0:2, :], bank[4][:, :].rearrange("p (i t) -> p i t", i=2), vT[:, 0:2, :], ALU.mult)
                TT(bonus[:, 2, :], bank[7][:, 0:T], vT[:, 2, :], ALU.mult).then_inc(bonus_ready, 1)
                dve.wait_ge(unit_done, UNIT0[l] + N_UNITS[l])
                for i in range(NRT):
                    STT(aT[:, i, :].rearrange("p (c t) -> p c t", c=NC),
                        kk[:, i, :].rearrange("p (c t) -> p c t", c=NC), -1.0, w65[:, i, :, 0:C],
                        ALU.mult, ALU.mult)
                TT(bT, a_gate, inv_w, ALU.mult).then_inc(rw_ready, 1)
                recurrence(l, 0)
                recurrence(l, 1)
                for m in range(KT):
                    dve.wait_ge(wo_done, 8 * l + m + 1)
                    TT(xT[:, m, :], xT[:, m, :], bank[m % 4][:, 0:T], ALU.add).then_inc(wo_added, 1)
                    if m == 5:
                        if l:
                            split("g", 0, 0)
                        else:
                            dense_split("g", 0)
                dve.wait_ge(wo_added, 8 * l + 8)
                norm(2 * l + 1, l, "ffn_norm")
                if l == 0:

                    def dense_multiply(j):
                        dve.wait_ge(ds_done, j + 1)
                        dve.wait_ge(pc_free, PIECES + 4 * (place_of[("u", j)] + 1))
                        if j:
                            dve.wait_ge(da_low, j)
                        for i in range(2):
                            cs = slice(i * 512, (i + 1) * 512)
                            last = TT(dense_act[:, cs], dense_sil[:, cs], bank[2 + i][:, :], ALU.mult)
                        last.then_inc(da_ready, 1)

                    def dense_low(j):
                        dve.wait_ge(da_ready, j + 1)
                        dve.wait_ge(da_high, j + 1)
                        TT(da_parts(j)[1], dense_act, da_parts(j)[0].bitcast(F32), ALU.subtract).then_inc(da_low, 1)

                    dense_split("u", 0)
                    dense_split("g", 1)
                    dense_multiply(0)
                    for j in range(1, NJ):
                        if j > 1:
                            dense_split("g", j)
                        dense_split("u", j)
                        dense_low(j - 1)
                        dense_split("d", j - 1)
                        dense_multiply(j)
                    dense_low(NJ - 1)
                    dense_split("d", NJ - 1)
                    dve.wait_ge(pc_free, PIECES + PIECES_E)
                    for i in range(4):
                        TT(xT[:, 2 * i:2 * i + 2, :], xT[:, 2 * i:2 * i + 2, :],
                           bank[4 + i][:, :].rearrange("p (k t) -> p k t", k=2), ALU.add).then_inc(x_ffn, 1)
                    dve.wait_ge(x_ffn, 4)

            def cols(at, n=16):
                return small[:, at:at + n]

            def per(ap):
                return ap.rearrange("p (b e) -> p b e", b=2)

            sel, logits, first, second, cand, gates = (cols(16 * n) for n in range(6))
            top1, top2, at_, g1, g2 = (cols(128 + 2 * n, 2) for n in range(5))
            rank, cmax = cols(144), cols(162, 1)
            e2 = top_gap
            iota8 = spread(const("iota")[:, 0:NE], 2)
            dve.wait_ge(logit_done, 1)
            then(TS(logits, bank[0][:, 0:16], 1.0, None, ALU.mult))

            def largest(value, hot):
                then(dve.tensor_reduce(value, per(logits), AX.X, ALU.max))
                then(TT(per(cand), per(logits), stretch(value, NE), ALU.not_equal))
                then(STT(per(cand), per(cand), float(NE), iota8, ALU.mult, ALU.add))
                then(dve.tensor_reduce(at_, per(cand), AX.X, ALU.min))
                then(TT(per(hot), iota8, stretch(at_, NE), ALU.is_equal))

            largest(top1, first)
            then(STT(logits, first, -3e38, logits, ALU.mult, ALU.add))
            largest(top2, second)
            TT(sel, first, second, ALU.add).then_inc(route_sel, 1)
            TT(e2, top2, top1, ALU.subtract).then_inc(route_act, 1)
            dve.wait_ge(rank_done, 1)
            then(STT(rank, bank[1][:, 0:16], 1.0, sel, ALU.add, ALU.mult))
            TS(rank, rank, -1.0, None, ALU.add)
            then(dve.tensor_reduce(cmax, bank[1][:, 16:24], AX.X, ALU.max))
            TS(flag[:, :], cmax, float(P), None, ALU.is_gt).then_inc(flag_ready, 1)
            dve.wait_ge(flag_ready, 1)

            def work_out_gates():
                dve.wait_ge(route_exp, 1)
                then(TS(g1, e2, 1.0, None, ALU.add))
                then(dve.reciprocal(g1, g1))
                then(TT(g2, e2, g1, ALU.mult))
                then(TT(per(gates), per(first), stretch(g1, NE), ALU.mult))
                then(TT(per(cand), per(second), stretch(g2, NE), ALU.mult))
                then(TT(gates, gates, cand, ALU.add))

            def moe_pass(p):
                if p:
                    then(TS(rank, rank, -float(P), None, ALU.add))
                hot16 = onehot.rearrange("p b e s -> p (b e) s")
                TT(hot16, spread(const("iota"), 2 * NE), stretch(rank, P), ALU.is_equal).then_inc(oh_ready, 1)
                dve.wait_ge(oh_ready, p + 1)
                if p == 0:
                    work_out_gates()
                TT(gated.rearrange("p b e s -> p (b e) s"), hot16, stretch(gates, P), ALU.mult).then_inc(gated_ready, 1)

                def gathered(at1):
                    for f in range(2):
                        dve.wait_ge(ga_kept, at1 * 2 + (f + 1))
                        fs = slice(f * CW, (f + 1) * CW)
                        TT(xg_lo[:, fs], bank[1 + 2 * f][:, :], xg_hi[:, fs].bitcast(F32), ALU.subtract).then_inc(
                            ga_low, 1)

                def multiply(j, at1):
                    dve.wait_ge(sl_done, at1 * NJ + (j + 1))
                    dve.wait_ge(pc_free, at1 * PIECES_E + (PIECES_E + 4 * (place_of[("u", j)] + 1) + PIECES))
                    if j >= 2:
                        dve.wait_ge(at_done, at1 * NJ + (j - 1))
                    TT(act_b[j % 2], sil_b[j % 2], bank[2 + j % 2][:, :], ALU.mult).then_inc(ac_ready, 1)

                def turned(j, at1):
                    dve.wait_ge(at_kept, at1 * NJ + (j + 1))
                    TT(at_lo[:, j % 2, :], bank[6][:, :], at_hi[:, j % 2, :].bitcast(F32), ALU.subtract).then_inc(
                        at_low, 1)

                def add(at1):
                    for f in range(4):
                        b, hf = f // 2, f % 2
                        dve.wait_ge(sct_done, at1 * 4 + (f + 1))
                        o = x_tok[:, b, hf * 512:(hf + 1) * 512]
                        TT(o, o, bank[(6, 7, 4, 5)[f]][:, :], ALU.add).then_inc(sct_added, 1)

                def expert(e, at1, last_one):
                    dve.tensor_copy(combine_e, combine[:, e, :]).then_inc(cbe_ready, 1)
                    split("g", 1, at1)
                    multiply(0, at1)
                    split("u", 1, at1)
                    turned(0, at1)
                    split("d", 0, at1)
                    for j in range(2, NJ):
                        multiply(j - 1, at1)
                        split("g", j, at1)
                        split("u", j, at1)
                        turned(j - 1, at1)
                        split("d", j - 1, at1)
                    multiply(NJ - 1, at1)
                    split("d", NJ - 1, at1, range(0, TURN_AT))
                    turned(NJ - 1, at1)
                    split("d", NJ - 1, at1, range(TURN_AT, 4))
                    if not last_one:
                        gathered(at1 + 1)
                        split("g", 0, at1 + 1)
                        split("u", 0, at1 + 1)
                    add(at1)
                    dve.wait_ge(sct_added, at1 * 4 + 4)

                first = p * NE
                gathered(first)
                if p:
                    split("g", 0, first)
                split("u", 0, first)
                dve.wait_ge(cb_kept, 4 * p + 4)
                dve.wait_ge(act_turned, 8)
                with dve.Fori(0, NE - 1) as e:
                    expert(e, e + first, False)
                expert(NE - 1, first + NE - 1, True)

            moe_pass(0)
            over_full = dve.value_load(flag[0:1, 0:1])
            with dve.If(over_full > 0):
                moe_pass(1)
            dve.memset(small[:, 0:1], 0.0).then_inc(moe_done, 1)


_OUT = "out"


def kernel(**inputs):
    import concourse.bacc as bacc
    from concourse.bass_utils import run_bass_kernel_spmd

    a = {k: np.asarray(v) for k, v in inputs.items()}

    def columns(v):
        return np.stack([r.reshape(-1, P).T for r in v.reshape(L, -1)])

    def twice(v):
        return np.concatenate([v, v], axis=1).reshape(L, P, 1)

    vres_rows = np.zeros((L, P, 4), np.float32)
    vres_rows[1, 0:16, 0] = a["vres_mu"][0]
    vres_rows[1, :, 1:4] = a["vres_v0"][0].reshape(NRT, P).T
    params = np.concatenate([
        columns(a["mix_norm"]), columns(a["tshift_mu"]), columns(a["decay_w0"]), columns(a["iclr_a0"]),
        columns(a["k_k"]), columns(a["k_a"]), columns(a["r_k"]), columns(a["ln_x_w"]), columns(a["ln_x_b"]),
        columns(a["conv_w"]), columns(a["conv_out_norm"]), twice(a["q_norm"]), twice(a["k_norm"]),
        columns(a["attn_out_norm"]), columns(a["ffn_norm"]), vres_rows], axis=2)
    assert params.shape[2] == N_PARAM
    consts, masks = constant_tables()
    arrays = {
        "x": a["x"][0], "consts": consts, "masks": masks,
        "params": np.ascontiguousarray(params.transpose(1, 0, 2)).reshape(P, L * N_PARAM),
        "lora": np.concatenate([a["decay_w2"], a["iclr_a2"], a["gate_g2"]], axis=1),
        "vres_v2": a["vres_v2"][0], "w_in": a["w_in"], "vres_w": a["vres_w_in"][0], "w_o": a["w_o"],
        "dense_wg": a["dense_wg"], "dense_wu": a["dense_wu"], "dense_wd": a["dense_wd"],
        "router": a["router"][0], "moe_wg": a["moe_wg"][0], "moe_wu": a["moe_wu"][0], "moe_wd": a["moe_wd"][0],
    }
    nc = bacc.Bacc("TRN2", target_bir_lowering=False, num_devices=1)
    feed, aps = {}, []
    for name, v in arrays.items():
        v = np.ascontiguousarray(v)
        feed["in_" + name] = v
        aps.append(nc.dram_tensor("in_" + name, v.shape, mybir.dt.from_np(v.dtype), kind="ExternalInput").ap())
    result = nc.dram_tensor(_OUT, (T, D), F32, kind="ExternalOutput").ap()
    decoder_trunk(nc, *aps, result)
    r = run_bass_kernel_spmd(nc, [feed], core_ids=[0])
    return r.results[0][_OUT].reshape(1, T, D)
```
